# Optimizing a Trainium2 kernel written in Bass

```python
import math
import jax
import jax.numpy as jnp
from jax import lax
import numpy as np

D_MODEL = 1024
BATCH = 1
SEQ = 256
DEPTH = 2

GRID_W = 64
CTX_LEN = 256
N_MIXERS = 4
GROUP_W = D_MODEL // N_MIXERS
MIX_W = N_MIXERS * GROUP_W
HEAD_DIM = 64
N_FOURIER = GROUP_W // HEAD_DIM
N_DIFF = GROUP_W // HEAD_DIM
DIFF_QK = HEAD_DIM // 2
DIFF_V = HEAD_DIM
N_NA = GROUP_W // HEAD_DIM
NA_KH_MAX = 8
NA_KW = 16
N_GMLP = GROUP_W // HEAD_DIM
CHUNK = 128
D_FF = 2816
CONV_W = 3
ROPE_BASE = 10000.0
Q_BLOCK = 128
EPS = 1e-6
IN_W = GROUP_W + 3 * GROUP_W + 3 * GROUP_W + 2 * GROUP_W


def rms_norm(x, g):
    xf = x.astype(jnp.float32)
    y = xf * lax.rsqrt(jnp.mean(xf * xf, axis=-1, keepdims=True) + EPS)
    return (y * g.astype(jnp.float32)).astype(x.dtype)

def axial_rope_tables(n, dim, dtype):
    n_freq = dim // 4
    freqs = ROPE_BASE ** (-jnp.arange(n_freq, dtype=jnp.float32) / n_freq)
    t = jnp.arange(n)
    row = (t // GRID_W).astype(jnp.float32)
    col = (t % GRID_W).astype(jnp.float32)
    ang = jnp.concatenate([row[:, None] * freqs, col[:, None] * freqs], axis=-1)
    return jnp.cos(ang).astype(dtype), jnp.sin(ang).astype(dtype)

def apply_rope(x, cos, sin):
    x1, x2 = jnp.split(x, 2, axis=-1)
    return jnp.concatenate([x1 * cos - x2 * sin, x1 * sin + x2 * cos], axis=-1)

def dense_attention(q, k, v):
    s = jnp.einsum('bhqd,bhkd->bhqk', q, k).astype(jnp.float32) * (q.shape[-1] ** -0.5)
    a = jax.nn.softmax(s, axis=-1).astype(v.dtype)
    return jnp.einsum('bhqk,bhkd->bhqd', a, v)

def fourier_mix(p):
    b, n, _ = p.shape
    g = p.reshape(b, n, N_FOURIER, HEAD_DIM).astype(jnp.float32)
    f = jnp.fft.fft2(g, axes=(1, 3), norm='ortho').real
    return f.reshape(b, n, GROUP_W).astype(p.dtype)

def diff_q(p, qn):
    b, n, _ = p.shape
    q = rms_norm(p[..., :GROUP_W].reshape(b, n, N_DIFF, 2, DIFF_QK), qn)
    return q.transpose(0, 2, 3, 1, 4)

def diff_kv(p, kn):
    b, n, _ = p.shape
    k = rms_norm(p[..., GROUP_W:2 * GROUP_W].reshape(b, n, N_DIFF, 2, DIFF_QK), kn)
    v = p[..., 2 * GROUP_W:].reshape(b, n, N_DIFF, DIFF_V)
    return k.transpose(0, 2, 3, 1, 4), v.transpose(0, 2, 1, 3)

def diff_core(q, k, v, lam):
    s = jnp.einsum('bhcqd,bhckd->bhcqk', q, k).astype(jnp.float32) * (DIFF_QK ** -0.5)
    a = jax.nn.softmax(s, axis=-1)
    w = (a[:, :, 0] - lam * a[:, :, 1]).astype(v.dtype)
    return jnp.einsum('bhqk,bhkd->bhqd', w, v)

def diff_finish(o, subln, lam_init):
    b, _, n, _ = o.shape
    o = rms_norm(o, subln) * (1.0 - lam_init)
    return o.transpose(0, 2, 1, 3).reshape(b, n, GROUP_W)

def diff_attention_latent(p, kc, vc, qn, kn, lam, subln, lam_init, cos, sin):
    b, n, _ = p.shape
    q = apply_rope(diff_q(p, qn), cos, sin)
    k, v = diff_kv(p, kn)
    k = apply_rope(k, cos, sin)
    k_all = jnp.concatenate([k, kc], axis=3)
    v_all = jnp.concatenate([v, vc], axis=2)
    nb = n // Q_BLOCK
    qb = jnp.moveaxis(q.reshape(b, N_DIFF, 2, nb, Q_BLOCK, DIFF_QK), 3, 0)
    o = lax.map(lambda qq: diff_core(qq, k_all, v_all, lam), qb)
    o = jnp.moveaxis(o, 0, 2).reshape(b, N_DIFF, n, DIFF_V)
    return diff_finish(o, subln, lam_init)

def na_q(p, qn):
    b, n, _ = p.shape
    return rms_norm(p[..., :GROUP_W].reshape(b, n, N_NA, HEAD_DIM), qn).transpose(0, 2, 1, 3)

def na_kv(p, kn):
    b, n, _ = p.shape
    k = rms_norm(p[..., GROUP_W:2 * GROUP_W].reshape(b, n, N_NA, HEAD_DIM), kn)
    v = p[..., 2 * GROUP_W:].reshape(b, n, N_NA, HEAD_DIM)
    return k.transpose(0, 2, 1, 3), v.transpose(0, 2, 1, 3)

def na_attention_latent(p, kc, vc, qn, kn, rpb):
    b, n, _ = p.shape
    rows = n // GRID_W
    kh = min(NA_KH_MAX, rows)
    n_loc = kh * NA_KW
    q = na_q(p, qn)
    k, v = na_kv(p, kn)
    r = jnp.arange(rows)
    r0 = jnp.clip(r - kh // 2, 0, rows - kh)
    row_off = r0[:, None] + jnp.arange(kh)[None, :] - r[:, None] + NA_KH_MAX - 1
    j = jnp.arange(GRID_W)
    c0 = jnp.clip(j - NA_KW // 2, 0, GRID_W - NA_KW)
    col_idx = c0[:, None] + jnp.arange(NA_KW)[None, :]
    col_off = col_idx - j[:, None] + NA_KW - 1
    rpb_c = rpb[:, :, col_off]
    kg = k.reshape(b, N_NA, rows, GRID_W, HEAD_DIM)
    vg = v.reshape(b, N_NA, rows, GRID_W, HEAD_DIM)
    scale = HEAD_DIM ** -0.5

    def row_block(args):
        qr, start, roff = args
        kr = lax.dynamic_slice_in_dim(kg, start, kh, axis=2)[:, :, :, col_idx]
        vr = lax.dynamic_slice_in_dim(vg, start, kh, axis=2)[:, :, :, col_idx]
        bias = jnp.transpose(rpb_c[:, roff], (0, 2, 1, 3)).astype(jnp.float32)
        s_loc = jnp.einsum('bhjd,bhajkd->bhjak', qr, kr).astype(jnp.float32) * scale + bias
        s_ctx = jnp.einsum('bhjd,bhcd->bhjc', qr, kc).astype(jnp.float32) * scale
        s = jnp.concatenate([s_loc.reshape(b, N_NA, GRID_W, n_loc), s_ctx], axis=-1)
        a = jax.nn.softmax(s, axis=-1).astype(vr.dtype)
        a_loc = a[..., :n_loc].reshape(b, N_NA, GRID_W, kh, NA_KW)
        return (jnp.einsum('bhjak,bhajkd->bhjd', a_loc, vr)
                + jnp.einsum('bhjc,bhcd->bhjd', a[..., n_loc:], vc))

    qg = jnp.moveaxis(q.reshape(b, N_NA, rows, GRID_W, HEAD_DIM), 2, 0)
    o = lax.map(row_block, (qg, r0, row_off))
    o = jnp.moveaxis(o, 0, 2).reshape(b, N_NA, n, HEAD_DIM)
    return o.transpose(0, 2, 1, 3).reshape(b, n, GROUP_W)

def na_attention_context(p, kc, vc, qn):
    b, n, _ = p.shape
    o = dense_attention(na_q(p, qn), kc, vc)
    return o.transpose(0, 2, 1, 3).reshape(b, n, GROUP_W)

def chunk_gmlp(p, gn, ws, bs):
    b, n, _ = p.shape
    u, v = jnp.split(jax.nn.gelu(p), 2, axis=-1)
    v = rms_norm(v.reshape(b, n // CHUNK, CHUNK, N_GMLP, HEAD_DIM), gn.reshape(N_GMLP, HEAD_DIM))
    s = jnp.einsum('gpq,bnqgc->bnpgc', ws, v) + jnp.swapaxes(bs, 0, 1)[:, :, None]
    return u * s.reshape(b, n, GROUP_W)

def conv_ffn(h, w_up, w_conv, b_conv, w_down):
    z = h @ w_up
    ch = z.shape[-1]
    z = lax.conv_general_dilated(z, w_conv[:, None, :].astype(z.dtype), window_strides=(1,),
                                 padding=((CONV_W // 2, CONV_W // 2),),
                                 dimension_numbers=('NWC', 'WIO', 'NWC'),
                                 feature_group_count=ch) + b_conv
    g, v = jnp.split(z, 2, axis=-1)
    return (jax.nn.silu(g) * v) @ w_down

def first_inputs(seed: int = 0) -> dict:
    key = jax.random.key(seed)
    ks = jax.random.split(key, 24)
    f32 = jnp.float32

    def nrm(k, shape, s):
        return jax.random.normal(k, shape, f32) * s

    def gain(k, shape):
        return 1.0 + 0.02 * jax.random.normal(k, shape, f32)

    return {
        "x": nrm(ks[0], (BATCH, SEQ, D_MODEL), 1.0),
        "c": nrm(ks[1], (BATCH, D_MODEL), 1.0),
        "ctx": nrm(ks[2], (BATCH, CTX_LEN, D_MODEL), 1.0),
        "c_ctx": nrm(ks[3], (D_MODEL,), 1.0),
        "w_ada": nrm(ks[4], (DEPTH, D_MODEL, 6 * D_MODEL), 0.5 * D_MODEL ** -0.5),
        "b_ada": nrm(ks[5], (DEPTH, 6 * D_MODEL), 0.02),
        "g_mix": gain(ks[6], (DEPTH, D_MODEL)),
        "g_ffn": gain(ks[7], (DEPTH, D_MODEL)),
        "w_in": nrm(ks[8], (DEPTH, D_MODEL, IN_W), D_MODEL ** -0.5),
        "w_out": nrm(ks[9], (DEPTH, MIX_W, D_MODEL), MIX_W ** -0.5),
        "diff_qn": gain(ks[10], (DEPTH, DIFF_QK)),
        "diff_kn": gain(ks[11], (DEPTH, DIFF_QK)),
        "diff_lam": nrm(ks[12], (DEPTH, 4, DIFF_QK), 0.1),
        "diff_subln": gain(ks[13], (DEPTH, DIFF_V)),
        "na_qn": gain(ks[14], (DEPTH, HEAD_DIM)),
        "na_kn": gain(ks[15], (DEPTH, HEAD_DIM)),
        "na_rpb": nrm(ks[16], (DEPTH, N_NA, 2 * NA_KH_MAX - 1, 2 * NA_KW - 1), 0.02),
        "gmlp_norm": gain(ks[17], (DEPTH, GROUP_W)),
        "gmlp_ws": nrm(ks[18], (DEPTH, N_GMLP, CHUNK, CHUNK), CHUNK ** -0.5),
        "gmlp_b": nrm(ks[19], (DEPTH, N_GMLP, CHUNK), 0.02),
        "ffn_up": nrm(ks[20], (DEPTH, D_MODEL, 2 * D_FF), D_MODEL ** -0.5),
        "ffn_conv": nrm(ks[21], (DEPTH, CONV_W, 2 * D_FF), CONV_W ** -0.5),
        "ffn_conv_b": nrm(ks[22], (DEPTH, 2 * D_FF), 0.02),
        "ffn_down": nrm(ks[23], (DEPTH, D_FF, D_MODEL), D_FF ** -0.5),
    }

def first_block(x, c, ctx, c_ctx, w_ada, b_ada, g_mix, g_ffn, w_in, w_out, diff_qn, diff_kn, diff_lam,
              diff_subln, na_qn, na_kn, na_rpb, gmlp_norm, gmlp_ws, gmlp_b, ffn_up, ffn_conv, ffn_conv_b,
              ffn_down):
    n = x.shape[1]
    G = GROUP_W
    cos, sin = axial_rope_tables(n, DIFF_QK, x.dtype)
    s_lat = jax.nn.silu(c)[:, None, :]
    s_ctx = jax.nn.silu(c_ctx)
    for li in range(DEPTH):
        ctx_out = li < DEPTH - 1
        lam_init = 0.8 - 0.6 * math.exp(-0.3 * li)
        lf = diff_lam[li].astype(jnp.float32)
        lam = jnp.exp(jnp.sum(lf[0] * lf[1])) - jnp.exp(jnp.sum(lf[2] * lf[3])) + lam_init
        m_lat = jnp.split(s_lat @ w_ada[li] + b_ada[li], 6, axis=-1)
        m_ctx = jnp.split(s_ctx @ w_ada[li] + b_ada[li], 6, axis=-1)

        h = rms_norm(x, g_mix[li]) * (1.0 + m_lat[1]) + m_lat[0]
        hc = rms_norm(ctx, g_mix[li]) * (1.0 + m_ctx[1]) + m_ctx[0]
        p = h @ w_in[li]
        pc = hc @ w_in[li]
        kc_d, vc_d = diff_kv(pc[..., G:4 * G], diff_kn[li])
        kc_n, vc_n = na_kv(pc[..., 4 * G:7 * G], na_kn[li])
        y = jnp.concatenate([
            fourier_mix(p[..., :G]),
            diff_attention_latent(p[..., G:4 * G], kc_d, vc_d, diff_qn[li], diff_kn[li], lam,
                                  diff_subln[li], lam_init, cos, sin),
            na_attention_latent(p[..., 4 * G:7 * G], kc_n, vc_n, na_qn[li], na_kn[li], na_rpb[li]),
            chunk_gmlp(p[..., 7 * G:], gmlp_norm[li], gmlp_ws[li], gmlp_b[li]),
        ], axis=-1)
        x = x + m_lat[2] * (y @ w_out[li])
        if ctx_out:
            yc = jnp.concatenate([
                fourier_mix(pc[..., :G]),
                diff_finish(diff_core(diff_q(pc[..., G:4 * G], diff_qn[li]), kc_d, vc_d, lam),
                            diff_subln[li], lam_init),
                na_attention_context(pc[..., 4 * G:7 * G], kc_n, vc_n, na_qn[li]),
                chunk_gmlp(pc[..., 7 * G:], gmlp_norm[li], gmlp_ws[li], gmlp_b[li]),
            ], axis=-1)
            ctx = ctx + m_ctx[2] * (yc @ w_out[li])

        h = rms_norm(x, g_ffn[li]) * (1.0 + m_lat[4]) + m_lat[3]
        x = x + m_lat[5] * conv_ffn(h, ffn_up[li], ffn_conv[li], ffn_conv_b[li], ffn_down[li])
        if ctx_out:
            hc = rms_norm(ctx, g_ffn[li]) * (1.0 + m_ctx[4]) + m_ctx[3]
            ctx = ctx + m_ctx[5] * conv_ffn(hc, ffn_up[li], ffn_conv[li], ffn_conv_b[li], ffn_down[li])
    return x


N_MIXERS_2 = 3
D_FF_2 = 4 * D_MODEL
NORM_EPS = 1e-6

DN_K_HEADS = 8
DN_V_HEADS = 16
DN_HEAD_K = 128
DN_HEAD_V = 128
DN_GROUP = DN_V_HEADS // DN_K_HEADS
DN_K_DIM = DN_K_HEADS * DN_HEAD_K
DN_V_DIM = DN_V_HEADS * DN_HEAD_V
DN_QKV_DIM = 2 * DN_K_DIM + DN_V_DIM
DN_IN_DIM = DN_QKV_DIM + DN_V_DIM + 4 * DN_V_HEADS
SHORT_CONV = 5
DN_CHUNK = 64

GLA_HEADS = 4
GLA_K_DIM = D_MODEL // 2
GLA_V_DIM = D_MODEL
GLA_HEAD_K = GLA_K_DIM // GLA_HEADS
GLA_HEAD_V = GLA_V_DIM // GLA_HEADS
GLA_GATE_RANK = 16
GLA_GATE_NORMALIZER = 16.0
GLA_IN_DIM = 2 * GLA_K_DIM + 2 * GLA_V_DIM + 2 * GLA_GATE_RANK
GLA_CHUNK = 64

ATTN_Q_HEADS = 8
ATTN_KV_HEADS = 2
ATTN_HEAD_DIM = 128
ATTN_GROUP = ATTN_Q_HEADS // ATTN_KV_HEADS
ATTN_Q_DIM = ATTN_Q_HEADS * ATTN_HEAD_DIM
ATTN_KV_DIM = ATTN_KV_HEADS * ATTN_HEAD_DIM
ATTN_IN_DIM = ATTN_Q_DIM + 2 * ATTN_KV_DIM
ROPE_THETA = 10000.0


F32 = jnp.float32

def rms_norm_2(x, g):
    xf = x.astype(F32)
    y = xf * lax.rsqrt(jnp.mean(xf * xf, axis=-1, keepdims=True) + NORM_EPS)
    return (y * g.astype(F32)).astype(x.dtype)

def l2_normalize(x):
    xf = x.astype(F32)
    return xf * lax.rsqrt(jnp.sum(xf * xf, axis=-1, keepdims=True) + NORM_EPS)

def modulate(h, shift, scale):
    return h * (1.0 + scale) + shift

def squared_relu_ffn(h, w1, w2):
    return jnp.square(jax.nn.relu(h @ w1)) @ w2

def short_conv(u, w):
    n = u.shape[1]
    pad = SHORT_CONV // 2
    up = jnp.pad(u, ((0, 0), (pad, pad), (0, 0)))
    out = up[:, 0:n] * w[:, 0]
    for tap in range(1, SHORT_CONV):
        out = out + up[:, tap:tap + n] * w[:, tap]
    return out

def to_chunks(t, chunk):
    b, h, n = t.shape[:3]
    t = t.reshape((b, h, n // chunk, chunk) + t.shape[3:])
    return jnp.moveaxis(t, 2, 0)

def from_chunks(t):
    t = jnp.moveaxis(t, 0, 2)
    b, h, nc, chunk = t.shape[:4]
    return t.reshape((b, h, nc * chunk) + t.shape[4:])

def time_flip(t):
    return jnp.flip(t, axis=2)

def identity(t):
    return t

def axial_rope_tables_2(n_rows):
    row = jnp.repeat(jnp.arange(n_rows), GRID_W).astype(F32)
    col = jnp.tile(jnp.arange(GRID_W), n_rows).astype(F32)
    axis_dim = ATTN_HEAD_DIM // 2
    inv_freq = jnp.power(ROPE_THETA, -jnp.arange(0, axis_dim, 2, dtype=F32) / axis_dim)
    ang_row = row[:, None] * inv_freq
    ang_col = col[:, None] * inv_freq
    return jnp.cos(ang_row), jnp.sin(ang_row), jnp.cos(ang_col), jnp.sin(ang_col)

def rotate_pairs(x, cos, sin):
    x1, x2 = jnp.split(x, 2, axis=-1)
    cs, sn = cos[:, None, :], sin[:, None, :]
    return jnp.concatenate([x1 * cs - x2 * sn, x1 * sn + x2 * cs], axis=-1)

def apply_axial_rope(x, tables):
    cos_r, sin_r, cos_c, sin_c = tables
    xf = x.astype(F32)
    half = ATTN_HEAD_DIM // 2
    y = jnp.concatenate([rotate_pairs(xf[..., :half], cos_r, sin_r),
                         rotate_pairs(xf[..., half:], cos_c, sin_c)], axis=-1)
    return y.astype(x.dtype)

def gated_delta_rule(q, k, v, g, beta, state):
    c = DN_CHUNK
    tri = jnp.tril(jnp.ones((c, c), dtype=bool))
    strict = jnp.tril(jnp.ones((c, c), dtype=bool), -1)
    eye = jnp.eye(c, dtype=F32)

    def step(s, xs):
        qc, kc, vc, gc, bc = xs
        qc = jnp.repeat(qc, DN_GROUP, axis=1)
        kc = jnp.repeat(kc, DN_GROUP, axis=1)
        gcum = jnp.cumsum(gc, axis=-1)
        decay = jnp.exp(jnp.where(tri, gcum[..., :, None] - gcum[..., None, :], -jnp.inf))
        kk = jnp.einsum('bhid,bhjd->bhij', kc, kc)
        m = jnp.where(strict, bc[..., :, None] * kk * decay, 0.0)
        rhs = jnp.concatenate([vc * bc[..., None], kc * (bc * jnp.exp(gcum))[..., None]], axis=-1)
        sol = lax.linalg.triangular_solve(eye + m, rhs, left_side=True, lower=True, unit_diagonal=True)
        u, w = sol[..., :DN_HEAD_V], sol[..., DN_HEAD_V:]
        v_new = u - jnp.einsum('bhid,bhdv->bhiv', w, s)
        a_qk = jnp.einsum('bhid,bhjd->bhij', qc, kc) * decay
        o = (jnp.einsum('bhid,bhdv->bhiv', qc * jnp.exp(gcum)[..., None], s)
             + jnp.einsum('bhij,bhjv->bhiv', a_qk, v_new))
        tail = jnp.exp(gcum[..., -1:] - gcum)
        s = (s * jnp.exp(gcum[..., -1])[..., None, None]
             + jnp.einsum('bhjd,bhjv->bhdv', kc * tail[..., None], v_new))
        return s, o

    xs = (to_chunks(q, c), to_chunks(k, c), to_chunks(v, c), to_chunks(g, c), to_chunks(beta, c))
    state, o = lax.scan(step, state, xs)
    return from_chunks(o), state

def gla_rule(q, k, v, gk, state):
    c = GLA_CHUNK
    tri = jnp.tril(jnp.ones((c, c), dtype=bool))[:, :, None]

    def step(s, xs):
        qc, kc, vc, gc = xs
        bcum = jnp.cumsum(gc, axis=-2)
        rel = jnp.exp(jnp.where(tri, bcum[..., :, None, :] - bcum[..., None, :, :], -jnp.inf))
        a_qk = jnp.einsum('bhid,bhjd,bhijd->bhij', qc, kc, rel)
        o = (jnp.einsum('bhij,bhjv->bhiv', a_qk, vc)
             + jnp.einsum('bhid,bhdv->bhiv', qc * jnp.exp(bcum), s))
        last = bcum[..., -1:, :]
        s = (s * jnp.exp(last[..., 0, :])[..., None]
             + jnp.einsum('bhjd,bhjv->bhdv', kc * jnp.exp(last - bcum), vc))
        return s, o

    xs = (to_chunks(q, c), to_chunks(k, c), to_chunks(v, c), to_chunks(gk, c))
    state, o = lax.scan(step, state, xs)
    return from_chunks(o), state

def deltanet_mixer(hx, hc, w_in, conv_w, a_log, dt_bias, norm_g, w_out, with_ctx_out):
    def project(h):
        bsz, n, _ = h.shape
        p = h @ w_in
        qkv = jax.nn.silu(short_conv(p[..., :DN_QKV_DIM], conv_w))
        z = p[..., DN_QKV_DIM:DN_QKV_DIM + DN_V_DIM]
        ab = p[..., DN_QKV_DIM + DN_V_DIM:].astype(F32)
        q = l2_normalize(qkv[..., :DN_K_DIM].reshape(bsz, n, DN_K_HEADS, DN_HEAD_K)) * DN_HEAD_K ** -0.5
        k = l2_normalize(qkv[..., DN_K_DIM:2 * DN_K_DIM].reshape(bsz, n, DN_K_HEADS, DN_HEAD_K))
        v = qkv[..., 2 * DN_K_DIM:].reshape(bsz, n, DN_V_HEADS, DN_HEAD_V).astype(F32)
        a = ab[..., :2 * DN_V_HEADS].reshape(bsz, n, 2, DN_V_HEADS)
        b = ab[..., 2 * DN_V_HEADS:].reshape(bsz, n, 2, DN_V_HEADS)
        g = -jnp.exp(a_log.astype(F32)) * jax.nn.softplus(a + dt_bias.astype(F32))
        beta = jax.nn.sigmoid(b)
        return (jnp.swapaxes(q, 1, 2), jnp.swapaxes(k, 1, 2), jnp.swapaxes(v, 1, 2),
                jnp.moveaxis(g, 1, -1), jnp.moveaxis(beta, 1, -1), z)

    qx, kx, vx, gx, bx, zx = project(hx)
    qc, kc, vc, gc, bc, zc = project(hc)
    bsz = hx.shape[0]
    out_x, out_c = [], []
    for d in range(2):
        flip = time_flip if d == 1 else identity
        state0 = jnp.zeros((bsz, DN_V_HEADS, DN_HEAD_K, DN_HEAD_V), F32)
        oc, state_c = gated_delta_rule(flip(qc), flip(kc), flip(vc), flip(gc[:, d]), flip(bc[:, d]), state0)
        ox, _ = gated_delta_rule(flip(qx), flip(kx), flip(vx), flip(gx[:, d]), flip(bx[:, d]), state_c)
        out_x.append(flip(ox))
        out_c.append(flip(oc))

    def readout(o, z):
        bsz_, n = z.shape[:2]
        o = rms_norm_2(jnp.swapaxes(o, 1, 2), norm_g)
        o = o * jax.nn.silu(z.reshape(bsz_, n, DN_V_HEADS, DN_HEAD_V).astype(F32))
        return o.reshape(bsz_, n, DN_V_DIM).astype(z.dtype) @ w_out

    yx = readout(out_x[0] + out_x[1], zx)
    yc = readout(out_c[0] + out_c[1], zc) if with_ctx_out else None
    return yx, yc

def gla_mixer(hx, hc, w_in, gate_w2, gate_b2, norm_g, w_out, with_ctx_out):
    def project(h):
        bsz, n, _ = h.shape
        p = h @ w_in
        q = p[..., :GLA_K_DIM].reshape(bsz, n, GLA_HEADS, GLA_HEAD_K).astype(F32) * GLA_HEAD_K ** -0.5
        k = p[..., GLA_K_DIM:2 * GLA_K_DIM].reshape(bsz, n, GLA_HEADS, GLA_HEAD_K).astype(F32)
        v = p[..., 2 * GLA_K_DIM:2 * GLA_K_DIM + GLA_V_DIM].reshape(bsz, n, GLA_HEADS, GLA_HEAD_V).astype(F32)
        gate = p[..., 2 * GLA_K_DIM + GLA_V_DIM:2 * GLA_K_DIM + 2 * GLA_V_DIM]
        low = p[..., 2 * GLA_K_DIM + 2 * GLA_V_DIM:].reshape(bsz, n, 2, GLA_GATE_RANK)
        logits = jnp.einsum('btdr,drk->btdk', low, gate_w2) + gate_b2
        gk = jax.nn.log_sigmoid(logits.astype(F32)) / GLA_GATE_NORMALIZER
        gk = gk.reshape(bsz, n, 2, GLA_HEADS, GLA_HEAD_K).transpose(0, 2, 3, 1, 4)
        return jnp.swapaxes(q, 1, 2), jnp.swapaxes(k, 1, 2), jnp.swapaxes(v, 1, 2), gk, gate

    qx, kx, vx, gx, zx = project(hx)
    qc, kc, vc, gc, zc = project(hc)
    bsz = hx.shape[0]
    out_x, out_c = [], []
    for d in range(2):
        flip = time_flip if d == 1 else identity
        state0 = jnp.zeros((bsz, GLA_HEADS, GLA_HEAD_K, GLA_HEAD_V), F32)
        oc, state_c = gla_rule(flip(qc), flip(kc), flip(vc), flip(gc[:, d]), state0)
        ox, _ = gla_rule(flip(qx), flip(kx), flip(vx), flip(gx[:, d]), state_c)
        out_x.append(flip(ox))
        out_c.append(flip(oc))

    def readout(o, z):
        bsz_, n = z.shape[:2]
        o = rms_norm_2(jnp.swapaxes(o, 1, 2), norm_g)
        o = o * jax.nn.silu(z.reshape(bsz_, n, GLA_HEADS, GLA_HEAD_V).astype(F32))
        return o.reshape(bsz_, n, GLA_V_DIM).astype(z.dtype) @ w_out

    yx = readout(out_x[0] + out_x[1], zx)
    yc = readout(out_c[0] + out_c[1], zc) if with_ctx_out else None
    return yx, yc

def attention_mixer(hx, hc, w_in, q_norm_g, k_norm_g, w_out, rope, with_ctx_out):
    def project(h):
        bsz, n, _ = h.shape
        p = h @ w_in
        q = p[..., :ATTN_Q_DIM].reshape(bsz, n, ATTN_Q_HEADS, ATTN_HEAD_DIM)
        k = p[..., ATTN_Q_DIM:ATTN_Q_DIM + ATTN_KV_DIM].reshape(bsz, n, ATTN_KV_HEADS, ATTN_HEAD_DIM)
        v = p[..., ATTN_Q_DIM + ATTN_KV_DIM:].reshape(bsz, n, ATTN_KV_HEADS, ATTN_HEAD_DIM)
        return rms_norm_2(q, q_norm_g), rms_norm_2(k, k_norm_g), v

    qx, kx, vx = project(hx)
    qc, kc, vc = project(hc)
    qx = apply_axial_rope(qx, rope)
    kx = apply_axial_rope(kx, rope)
    bsz, n = hx.shape[:2]
    scale = ATTN_HEAD_DIM ** -0.5

    def attend(q_blk, keys, values):
        s = jnp.einsum('bkgqd,bksd->bkgqs', q_blk, keys).astype(F32) * scale
        p = jax.nn.softmax(s, axis=-1).astype(values.dtype)
        return jnp.einsum('bkgqs,bksd->bkgqd', p, values)

    k_all = jnp.concatenate([kx, kc], axis=1).transpose(0, 2, 1, 3)
    v_all = jnp.concatenate([vx, vc], axis=1).transpose(0, 2, 1, 3)
    n_blk = n // Q_BLOCK
    q_blocks = qx.reshape(bsz, n_blk, Q_BLOCK, ATTN_KV_HEADS, ATTN_GROUP, ATTN_HEAD_DIM).transpose(1, 0, 3, 4, 2, 5)
    o = lax.map(lambda qb: attend(qb, k_all, v_all), q_blocks)
    yx = o.transpose(1, 0, 4, 2, 3, 5).reshape(bsz, n, ATTN_Q_DIM) @ w_out
    yc = None
    if with_ctx_out:
        lc = hc.shape[1]
        q_ctx = qc.reshape(bsz, lc, ATTN_KV_HEADS, ATTN_GROUP, ATTN_HEAD_DIM).transpose(0, 2, 3, 1, 4)
        oc = attend(q_ctx, kc.transpose(0, 2, 1, 3), vc.transpose(0, 2, 1, 3))
        yc = oc.transpose(0, 3, 1, 2, 4).reshape(bsz, lc, ATTN_Q_DIM) @ w_out
    return yx, yc

def second_inputs(seed: int = 0) -> dict:
    key = jax.random.key(seed)
    ks = jax.random.split(key, 32)
    n_a = len(range(0, DEPTH, N_MIXERS_2))
    n_b = len(range(1, DEPTH, N_MIXERS_2))
    n_c = len(range(2, DEPTH, N_MIXERS_2))

    def normal(k, shape, scale):
        return jax.random.normal(k, shape, F32) * scale

    def gain(k, shape):
        return 1.0 + normal(k, shape, 0.02)

    dt = jnp.exp(jax.random.uniform(ks[12], (n_a, 2, DN_V_HEADS), F32, math.log(1e-3), math.log(1e-1)))
    return {
        'x': normal(ks[0], (BATCH, SEQ, D_MODEL), 1.0),
        'c': normal(ks[1], (BATCH, D_MODEL), 1.0),
        'ctx': normal(ks[2], (BATCH, CTX_LEN, D_MODEL), 1.0),
        'c_ctx': normal(ks[3], (D_MODEL,), 1.0),
        'ada_w': normal(ks[4], (DEPTH, D_MODEL, 6 * D_MODEL), 0.5 * D_MODEL ** -0.5),
        'ada_b': normal(ks[5], (DEPTH, 6 * D_MODEL), 0.01),
        'norm_mix_g': gain(ks[6], (DEPTH, D_MODEL)),
        'norm_ffn_g': gain(ks[7], (DEPTH, D_MODEL)),
        'ffn_w1': normal(ks[8], (DEPTH, D_MODEL, D_FF_2), D_MODEL ** -0.5),
        'ffn_w2': normal(ks[9], (DEPTH, D_FF_2, D_MODEL), D_FF_2 ** -0.5),
        'dn_w_in': normal(ks[10], (n_a, D_MODEL, DN_IN_DIM), D_MODEL ** -0.5),
        'dn_conv_w': normal(ks[11], (n_a, DN_QKV_DIM, SHORT_CONV), SHORT_CONV ** -0.5),
        'dn_a_log': jnp.log(jax.random.uniform(ks[13], (n_a, 2, DN_V_HEADS), F32, 1.0, 16.0)),
        'dn_dt_bias': dt + jnp.log(-jnp.expm1(-dt)),
        'dn_norm_g': gain(ks[14], (n_a, DN_HEAD_V)),
        'dn_w_out': normal(ks[15], (n_a, DN_V_DIM, D_MODEL), DN_V_DIM ** -0.5),
        'gla_w_in': normal(ks[16], (n_b, D_MODEL, GLA_IN_DIM), D_MODEL ** -0.5),
        'gla_gate_w2': normal(ks[17], (n_b, 2, GLA_GATE_RANK, GLA_K_DIM), GLA_GATE_RANK ** -0.5),
        'gla_gate_b2': normal(ks[18], (n_b, 2, GLA_K_DIM), 0.1),
        'gla_norm_g': gain(ks[19], (n_b, GLA_HEAD_V)),
        'gla_w_out': normal(ks[20], (n_b, GLA_V_DIM, D_MODEL), GLA_V_DIM ** -0.5),
        'attn_w_in': normal(ks[21], (n_c, D_MODEL, ATTN_IN_DIM), D_MODEL ** -0.5),
        'attn_q_norm_g': gain(ks[22], (n_c, ATTN_HEAD_DIM)),
        'attn_k_norm_g': gain(ks[23], (n_c, ATTN_HEAD_DIM)),
        'attn_w_out': normal(ks[24], (n_c, ATTN_Q_DIM, D_MODEL), ATTN_Q_DIM ** -0.5),
    }

def second_block(x, c, ctx, c_ctx, ada_w, ada_b, norm_mix_g, norm_ffn_g, ffn_w1, ffn_w2,
              dn_w_in, dn_conv_w, dn_a_log, dn_dt_bias, dn_norm_g, dn_w_out,
              gla_w_in, gla_gate_w2, gla_gate_b2, gla_norm_g, gla_w_out,
              attn_w_in, attn_q_norm_g, attn_k_norm_g, attn_w_out):
    n_tok = x.shape[1]
    ROWS = n_tok // GRID_W
    rope = axial_rope_tables_2(ROWS)
    for i in range(DEPTH):
        with_ctx_out = i < DEPTH - 1
        mix, slot = i % N_MIXERS_2, i // N_MIXERS_2
        mod_x = jnp.split((jax.nn.silu(c) @ ada_w[i] + ada_b[i])[:, None, :], 6, axis=-1)
        mod_c = jnp.split(jax.nn.silu(c_ctx) @ ada_w[i] + ada_b[i], 6, axis=-1)
        hx = modulate(rms_norm_2(x, norm_mix_g[i]), mod_x[0], mod_x[1])
        hc = modulate(rms_norm_2(ctx, norm_mix_g[i]), mod_c[0], mod_c[1])
        if mix == 0:
            yx, yc = deltanet_mixer(hx, hc, dn_w_in[slot], dn_conv_w[slot], dn_a_log[slot], dn_dt_bias[slot],
                                    dn_norm_g[slot], dn_w_out[slot], with_ctx_out)
        elif mix == 1:
            yx, yc = gla_mixer(hx, hc, gla_w_in[slot], gla_gate_w2[slot], gla_gate_b2[slot],
                               gla_norm_g[slot], gla_w_out[slot], with_ctx_out)
        else:
            yx, yc = attention_mixer(hx, hc, attn_w_in[slot], attn_q_norm_g[slot], attn_k_norm_g[slot],
                                     attn_w_out[slot], rope, with_ctx_out)
        x = x + mod_x[2] * yx
        hx = modulate(rms_norm_2(x, norm_ffn_g[i]), mod_x[3], mod_x[4])
        x = x + mod_x[5] * squared_relu_ffn(hx, ffn_w1[i], ffn_w2[i])
        if with_ctx_out:
            ctx = ctx + mod_c[2] * yc
            hc = modulate(rms_norm_2(ctx, norm_ffn_g[i]), mod_c[3], mod_c[4])
            ctx = ctx + mod_c[5] * squared_relu_ffn(hc, ffn_w1[i], ffn_w2[i])
    return x


def setup_inputs(seed=0):
    out = dict(first_inputs(seed))
    for name, value in second_inputs(seed + 1).items():
        if name != "x":
            out[name + "_2"] = value
    return out


def reference(
    x, c, ctx, c_ctx, w_ada, b_ada, g_mix, g_ffn, w_in, w_out, diff_qn, diff_kn, diff_lam,
    diff_subln, na_qn, na_kn, na_rpb, gmlp_norm, gmlp_ws, gmlp_b, ffn_up, ffn_conv, ffn_conv_b,
    ffn_down, c_2, ctx_2, c_ctx_2, ada_w_2, ada_b_2, norm_mix_g_2, norm_ffn_g_2, ffn_w1_2,
    ffn_w2_2, dn_w_in_2, dn_conv_w_2, dn_a_log_2, dn_dt_bias_2, dn_norm_g_2, dn_w_out_2,
    gla_w_in_2, gla_gate_w2_2, gla_gate_b2_2, gla_norm_g_2, gla_w_out_2, attn_w_in_2,
    attn_q_norm_g_2, attn_k_norm_g_2, attn_w_out_2,
):
    x = first_block(
        x, c, ctx, c_ctx, w_ada, b_ada, g_mix, g_ffn, w_in, w_out, diff_qn, diff_kn, diff_lam,
        diff_subln, na_qn, na_kn, na_rpb, gmlp_norm, gmlp_ws, gmlp_b, ffn_up, ffn_conv,
        ffn_conv_b, ffn_down,
    )
    return second_block(
        x, c_2, ctx_2, c_ctx_2, ada_w_2, ada_b_2, norm_mix_g_2, norm_ffn_g_2, ffn_w1_2,
        ffn_w2_2, dn_w_in_2, dn_conv_w_2, dn_a_log_2, dn_dt_bias_2, dn_norm_g_2, dn_w_out_2,
        gla_w_in_2, gla_gate_w2_2, gla_gate_b2_2, gla_norm_g_2, gla_w_out_2, attn_w_in_2,
        attn_q_norm_g_2, attn_k_norm_g_2, attn_w_out_2,
    )


_drawn_inputs = setup_inputs


def setup_inputs(seed=0):
    import zlib

    import numpy as np

    out = dict(_drawn_inputs(seed))
    spreads = {}
    factors = {'g_mix': 8.0,
     'g_ffn': 5.98,
     'diff_qn': 8.0,
     'diff_kn': 8.0,
     'diff_subln': 38.549,
     'na_qn': 8.0,
     'na_kn': 8.0,
     'na_rpb': 64.0,
     'gmlp_norm': 8.0,
     'gmlp_b': 8.0,
     'ffn_conv_b': 6.5,
     'norm_mix_g_2': 6.658,
     'norm_ffn_g_2': 17.456,
     'dn_norm_g_2': 26.63,
     'gla_gate_b2_2': 6.503,
     'gla_norm_g_2': 48.032}
    for name, (base, spread) in spreads.items():
        noise = np.random.default_rng([zlib.crc32(name.encode()), seed]).standard_normal(out[name].shape)
        drawn = base * np.exp(spread * noise) if base else spread * noise
        out[name] = jnp.asarray(drawn.astype(out[name].dtype))
    for name, factor in factors.items():
        out[name] = (out[name] * factor).astype(out[name].dtype)
    return out
```

```python
import math
from contextlib import ExitStack

import numpy as np
import concourse.bass as bass
from concourse import mybir

F32 = mybir.dt.float32
ALU = mybir.AluOpType
ACT = mybir.ActivationFunctionType
AX = mybir.AxisListType

D = 1024
KT = D // 128
SEQ = 256
TOK = 2 * SEQ
DEPTH = 2
GRID_W = 64
EPS = 1e-6
RING = 4
CHUNK_COLS = 256
CHUNK = KT * CHUNK_COLS
D_FF = 2816
FT = D_FF // 128
PAIRS = FT // 2
D_FF2 = 4096
FT2 = D_FF2 // 128
HEAD = 64
DIFF_QK = 32
NEG = -1.0e30
RPB_W = 31
RPB_H = 15
DELTA_C = 128
LEVELS = 7


def _offsets(sizes):
    at, out = 0, {}
    for name, size in sizes:
        out[name] = at
        at += size
    out["end"] = at
    return out


VEC_SIZES = [("c", 4 * KT)]
for _li in range(DEPTH):
    VEC_SIZES += [(f"b_ada{_li}", 48), (f"g_mix{_li}", KT), (f"g_ffn{_li}", KT), (f"conv{_li}", PAIRS * 16),
                  (f"qk{_li}", 8), (f"subln{_li}", 1), (f"gmlp_norm{_li}", 2)]
for _li in range(DEPTH):
    VEC_SIZES += [(f"ada_b_2{_li}", 48), (f"norm_mix_2{_li}", KT), (f"norm_ffn_2{_li}", KT)]
VEC_SIZES += [("dn_conv", 32 * 5), ("dn_norm", 1), ("gla_norm", 2)]
VEC = _offsets(VEC_SIZES)

C1_SIZES = [("blk32", 128), ("blk64", 128), ("rope", 128), ("cos", 256), ("sin", 256), ("dft_n", 1024),
            ("dft_c", 128), ("dft_s", 128), ("namask", 64)]
C1 = _offsets(C1_SIZES)
D1_SIZES = [("lam0", 128), ("lam1", 128), ("ws0", 512), ("ws1", 512), ("gb0", 256), ("gb1", 256)]
D1 = _offsets(D1_SIZES)

ADA_CHUNKS = 6 * D // CHUNK_COLS
ADA_GROUPS = ADA_CHUNKS // 2
IN1_CHUNKS = 9
OUT_CHUNKS = D // CHUNK_COLS
UP_CHUNKS = 2 * D_FF // CHUNK_COLS
FT_GROUPS = -(-FT // KT)
BLOCK1_CHUNKS = ADA_CHUNKS + IN1_CHUNKS + OUT_CHUNKS + UP_CHUNKS + OUT_CHUNKS * FT_GROUPS
NEXT_ADA = ("1ada1", "2ada0")
SLOT_ORDER = "fourier q k v q k v u v"
TOKEN_MAJOR = (0, 3, 6, 8)


def build_program(nc, t, out, BLOCKS=2):
    ctx = ExitStack()
    with ctx:
        def sb(name, cols):
            return ctx.enter_context(nc.sbuf_tensor(name, [128, cols], F32))

        def sems(names):
            return {n: ctx.enter_context(nc.semaphore(n)) for n in names.split()}

        ring = sb("ring", RING * CHUNK)
        x_sb = sb("x_sb", KT * TOK)
        h_sb = sb("h_sb", KT * TOK)
        arena = sb("arena", 28672)
        vec = sb("vec", VEC["end"])
        ones = sb("ones", 128)
        ident = sb("ident", 128)
        silu_c = sb("silu_c", 4 * KT)
        mods = sb("mods", 96)
        amul = sb("amul", 4 * KT)
        rinv = sb("rinv", TOK)
        small = sb("small", 128)
        psum = ctx.enter_context(nc.psum_tensor("psum", [128, 8 * 512], F32))

        w = ring[:, :].rearrange("p (r k c) -> p r k c", r=RING, k=KT)
        x = x_sb[:, :].rearrange("p (k t) -> p k t", k=KT)
        h = h_sb[:, :].rearrange("p (k t) -> p k t", k=KT)
        silu = silu_c[:, :].rearrange("p (b k s) -> p b k s", b=2, k=KT)
        mod = mods[:, :].rearrange("p (m s) -> p m s", s=2)
        a_mul = amul[:, :].rearrange("p (n k s) -> p n k s", n=2, k=KT)
        eps = small[:, 0:1]

        def bank(b, n=1):
            return psum[:, b * 512:(b + n) * 512]

        def v(name, n=1, at=0):
            return vec[:, VEC[name] + at:VEC[name] + at + n]

        def area(at, n, **dims):
            a = arena[:, at:at + n]
            if dims:
                names = " ".join(dims)
                a = a.rearrange(f"p ({names} z) -> p {names} z", **dims)
            return a

        def spread(ap, n, axis):
            ap = ap.unsqueeze(axis)
            shape = list(ap.shape)
            shape[axis] = n
            return ap.to_broadcast(shape)

        P = area(0, 18 * 512, s=18)
        y = area(9216, 8 * 512, k=8)
        SCR = area(13312, 4096)
        EXPO = area(17408, 2048, z2=2, c=2)
        WT = area(19456, 1024, z2=2, k=4)
        NAB = area(20480, 2048, h=4, q=2)
        CONST1 = 22528
        DATA1 = CONST1 + C1["end"]
        assert DATA1 + D1["end"] <= 28672

        def c1(name, n=128):
            return arena[:, CONST1 + C1[name]:CONST1 + C1[name] + n]

        def d1(name, n):
            return arena[:, DATA1 + D1[name]:DATA1 + D1[name] + n]

        act1 = area(0, FT * 512, k=FT)
        Z = area(FT * 512, 2048, q=4)
        ZE = area(FT * 512 + 2048, 1024, q=2)
        assert FT * 512 + 3072 <= 20480

        S = sems("""slot0 slot1 slot2 slot3 products bank_free loaded_vec loaded_x loaded_c1 loaded_nab
                    silu_tanh silu_ready ada_copied ada_turned next_copied next_turned mods_ready stored
                    n_sq n_sum n_rinv n_normed h_ready
                    g_in g_tanh g_done qk_sq qk_sum qk_rinv qk_normed rot_ready qk_ready lam_in lam_exp
                    f_cols f_copied f_rows gm_sq gm_rinv gm_ready gm_prod gm_done
                    scores_ready max_ready exp_done weights_ready wt_psum wt_ready o_ready o_copied
                    sub_sq sub_sum sub_rinv y_ready
                    z_init conv_done sig_tanh act_ready x_done""")
        slot_sem = [S[f"slot{i}"] for i in range(RING)]

        n_chunks = t["stream"].shape[0]
        at = {"chunk": 0, "result": 0}
        sched = {}

        def plan(name, chunks, results):
            sched[name] = (at["chunk"], at["result"])
            at["chunk"] += chunks
            at["result"] += results

        for li in range(DEPTH):
            if li == 0:
                plan("1ada0", ADA_CHUNKS, 0)
            plan(f"1in{li}", IN1_CHUNKS, 2 * IN1_CHUNKS)
            plan(NEXT_ADA[li], ADA_CHUNKS, 0)
            plan(f"1out{li}", OUT_CHUNKS, KT)
            plan(f"1up{li}", UP_CHUNKS, 2 * UP_CHUNKS)
            plan(f"1down{li}", OUT_CHUNKS * FT_GROUPS, KT)
        if BLOCKS == 2:
            plan_second(plan)
        total_chunks = at["chunk"]
        assert total_chunks <= n_chunks

        B = dict(locals())
        second = SecondBlock(B) if BLOCKS == 2 else None

        def arrived(pe, n, extra=None):
            value = 16 * (n // RING + 1)
            pe.wait_ge(slot_sem[n % RING], value if extra is None else 16 * extra + value)

        def k_products(pe, out_ap, lhs, rhs, nk=KT, first=True, last=True):
            for k in range(nk):
                ins = pe.matmul(out_ap, lhs(k), rhs(k), start=first and k == 0, stop=last and k == nk - 1)
            ins.then_inc(S["products"], 1)

        def pe_ada(pe, name, blk, inst):
            n0, _ = sched[name]
            if inst == 0:
                pe.wait_ge(S["silu_ready"], 1)

            def turn(g):
                pe.wait_ge(S["ada_copied"], ADA_GROUPS * inst + g + 1)
                rows = h_sb[0:2, 512 * (g % 2):512 * (g % 2) + 512]
                for m in range(4):
                    ins = pe.transpose(bank(6)[:, 2 * (4 * g + m):2 * (4 * g + m) + 2], rows[:, 128 * m:128 * (m + 1)],
                                       ident[0:2, 0:2])
                ins.then_inc(S["ada_turned"], 1)

            for g in range(ADA_GROUPS):
                if g >= 2:
                    pe.wait_ge(S["ada_copied"], ADA_GROUPS * inst + g - 1)
                for c in range(2):
                    n = n0 + 2 * g + c
                    arrived(pe, n)
                    for half in range(2):
                        for k in range(half * KT // 2, (half + 1) * KT // 2):
                            ins = pe.matmul(bank(4 + g % 2)[0:2, c * 256:(c + 1) * 256], silu[:, blk, k, :],
                                            w[:, n % RING, k, :], start=k == 0, stop=k == KT - 1)
                        ins.then_inc(S["products"], 1)
                if g >= 1:
                    turn(g - 1)
            turn(ADA_GROUPS - 1)

        def act_ada(act, name, inst):
            n0, _ = sched[name]
            for g in range(ADA_GROUPS):
                act.wait_ge(S["products"], 2 * n0 + 4 * (g + 1))
                if g >= 2:
                    act.wait_ge(S["ada_turned"], ADA_GROUPS * inst + g - 1)
                act.copy(h_sb[0:2, 512 * (g % 2):512 * (g % 2) + 512], bank(4 + g % 2)[0:2, :])\
                   .then_inc(S["ada_copied"], 1)

        def pe_norm(pe, k):
            pe.wait_ge(S["n_sq"], k + 1)
            for kt in range(KT):
                ins = pe.matmul(bank(5), ones[:, :], h[:, kt, :], start=kt == 0, stop=kt == KT - 1)
            ins.then_inc(S["n_sum"], 1)

        def in1_tokens(li, c):
            return SEQ if li == DEPTH - 1 and c in (1, 4, 7) else TOK

        def pe_in1(pe, li):
            n0, r0 = sched[f"1in{li}"]
            pe.wait_ge(S["h_ready"], KT * (2 * li + 1))
            for c in range(IN1_CHUNKS):
                arrived(pe, n0 + c)
                for half in range(2):
                    rho = 2 * c + half
                    if rho >= 4:
                        pe.wait_ge(S["bank_free"], r0 + rho - 3)
                    slot = (n0 + c) % RING
                    if c in TOKEN_MAJOR:
                        for tt in range(2):
                            tok = half * SEQ + tt * 128
                            for k in range(KT):
                                ins = pe.matmul(bank(rho % 4)[:, tt * 256:(tt + 1) * 256], h[:, k, tok:tok + 128],
                                                w[:, slot, k, :], start=k == 0, stop=k == KT - 1)
                        ins.then_inc(S["products"], 1)
                    else:
                        tok = in1_tokens(li, c)
                        k_products(pe, bank(rho % 4)[:, 0:tok], lambda k: w[:, slot, k, half * 128:(half + 1) * 128],
                                   lambda k: h[:, k, 0:tok])

        def pe_residual(pe, name, src, groups, kts, tok):
            n0, r0 = sched[name]
            n = n0
            for cp in range(OUT_CHUNKS):
                for g in range(groups):
                    arrived(pe, n)
                    for half in range(2):
                        rho = 2 * cp + half
                        if g == 0 and rho >= 4:
                            pe.wait_ge(S["bank_free"], r0 + rho - 3)
                        k_products(pe, bank(rho % 4)[:, 0:tok],
                                   lambda k: w[:, n % RING, k, half * 128:(half + 1) * 128],
                                   lambda k: src[:, g * KT + k, 0:tok],
                                   nk=min(KT, kts - g * KT), first=g == 0, last=g == groups - 1)
                    n += 1

        def dve_residual(dve, name, groups, gate, streams):
            n0, r0 = sched[name]
            for rho in range(KT):
                cp, half = divmod(rho, 2)
                dve.wait_ge(S["products"], 2 * (n0 + cp * groups + groups - 1) + half + 1)
                for s in range(streams):
                    part = x[:, rho, s * SEQ:(s + 1) * SEQ]
                    ins = dve.scalar_tensor_tensor(part, bank(rho % 4)[:, s * SEQ:(s + 1) * SEQ],
                                                   mod[:, gate * KT + rho, s:s + 1], part, ALU.mult, ALU.add)
                ins.then_inc(S["bank_free"], 1)
            dve.drain()

        def pe_attention(pe, li, units, u0):
            def scores(u):
                kind, st, hd, qt = units[u]
                g = u0 + u
                if u >= 2:
                    pe.wait_ge(S["exp_done"], g - 1)
                keys = P[:, (4 if kind == "diff" else 10) + hd // 2, st * SEQ:TOK]
                queries = P[:, (2 if kind == "diff" else 8) + hd // 2, st * SEQ + qt * 128:st * SEQ + qt * 128 + 128]
                width, count = (32, 2) if kind == "diff" else (64, 1)
                for c in range(count):
                    p = (hd % 2) * 64 + c * 32
                    ins = pe.matmul(bank(2 * (u % 2) + c)[:, 0:TOK - st * SEQ], queries[p:p + width], keys[p:p + width],
                                    start=True, stop=True)
                ins.then_inc(S["scores_ready"], 1)

            def transposes(u):
                kind, st, hd, qt = units[u]
                g = u0 + u
                pe.wait_ge(S["weights_ready"], g + 1)
                if u >= 2:
                    pe.wait_ge(S["wt_ready"], g - 1)
                nk = 4 - 2 * st
                for k in range(nk):
                    ins = pe.transpose(bank(4 + u % 2)[:, k * 128:(k + 1) * 128],
                                       EXPO[:, u % 2, 0, k * 128:(k + 1) * 128], ident[:, :])
                ins.then_inc(S["wt_psum"], 1)

            def values(u):
                kind, st, hd, qt = units[u]
                g = u0 + u
                pe.wait_ge(S["wt_ready"], g + 1)
                if u >= 1:
                    pe.wait_ge(S["o_copied"], g)
                nk = 4 - 2 * st
                vs = 6 if kind == "diff" else 12
                p = (hd % 2) * 64
                for k in range(nk):
                    kt = 2 * st + k
                    ins = pe.matmul(bank(6)[p:p + 64, 0:128],
                                    P[:, vs + kt // 2, (kt % 2) * 256 + hd * 64:(kt % 2) * 256 + hd * 64 + 64],
                                    WT[:, u % 2, k, :], start=k == 0, stop=k == nk - 1)
                ins.then_inc(S["o_ready"], 1)

            n = len(units)
            for u in range(n + 2):
                if u < n:
                    scores(u)
                if 1 <= u <= n:
                    transposes(u - 1)
                if u >= 2:
                    values(u - 2)
                for idx in next_ada_at(u, n):
                    pe_next_ada(pe, li, idx)
            pe_next_ada(pe, li, ADA_CHUNKS)

        def next_ada_at(u, units):
            per = -(-ADA_CHUNKS // units)
            return range(min(per * u, ADA_CHUNKS), min(per * (u + 1), ADA_CHUNKS))

        def pe_next_ada(pe, li, idx):
            n = sched[NEXT_ADA[li]][0] + idx
            at = ADA_CHUNKS * li + idx
            rows, turned = bank(7)[0:2, 0:256], bank(7)[:, 256:352]
            if idx >= 1:
                pe.wait_ge(S["next_copied"], at)
                for m in range(2):
                    col = 4 * (idx - 1) + 2 * m
                    ins = pe.transpose(turned[:, col:col + 2],
                                       h_sb[0:2, 256 * ((idx - 1) % 2) + 128 * m:256 * ((idx - 1) % 2) + 128 * (m + 1)],
                                       ident[0:2, 0:2])
                ins.then_inc(S["next_turned"], 1)
            if idx < ADA_CHUNKS:
                arrived(pe, n)
                for half in range(2):
                    for k in range(half * KT // 2, (half + 1) * KT // 2):
                        ins = pe.matmul(rows, silu[:, li, k, :], w[:, n % RING, k, :], start=k == 0, stop=k == KT - 1)
                    ins.then_inc(S["products"], 1)

        def act_next_ada(act, li, idx):
            n = sched[NEXT_ADA[li]][0] + idx
            act.wait_ge(S["products"], 2 * (n + 1))
            if idx >= 2:
                act.wait_ge(S["next_turned"], ADA_CHUNKS * li + idx - 1)
            act.copy(h_sb[0:2, 256 * (idx % 2):256 * (idx % 2) + 256], bank(7)[0:2, 0:256]).then_inc(S["next_copied"], 1)

        def act_attention(act, li, units, u0):
            def exponentials(u):
                kind, st, hd, qt = units[u]
                g = u0 + u
                act.wait_ge(S["max_ready"], g + 1)
                if u >= 2:
                    act.wait_ge(S["wt_psum"], g - 1)
                n = TOK - st * SEQ
                count = 2 if kind == "diff" else 1
                for c in range(count):
                    ins = act.activation(EXPO[:, u % 2, c, 0:n], bank(2 * (u % 2) + c)[:, 0:n], ACT.Exp,
                                         bias=small[:, 8 + 2 * (u % 2) + c:9 + 2 * (u % 2) + c],
                                         accum_out=small[:, 12 + 2 * (u % 2) + c:13 + 2 * (u % 2) + c])
                ins.then_inc(S["exp_done"], 1)

            def copy_wt(u):
                kind, st, hd, qt = units[u]
                g = u0 + u
                act.wait_ge(S["wt_psum"], g + 1)
                if u >= 2:
                    act.wait_ge(S["o_ready"], g - 1)
                nk = 4 - 2 * st
                act.copy(WT[:, u % 2, 0:nk, :], bank(4 + u % 2)[:, 0:nk * 128].rearrange("p (k q) -> p k q", k=nk))\
                   .then_inc(S["wt_ready"], 1)

            n = len(units)
            for u in range(n + 1):
                if u < n:
                    exponentials(u)
                if u >= 1:
                    copy_wt(u - 1)
                for idx in next_ada_at(u, n):
                    act_next_ada(act, li, idx)

        def dve_attention(dve, li, units, u0):
            neg_lam = small[:, 4:5]

            def maxima(u):
                kind, st, hd, qt = units[u]
                g = u0 + u
                dve.wait_ge(S["scores_ready"], g + 1)
                b = 2 * (u % 2)
                n = TOK - st * SEQ
                count = 2 if kind == "diff" else 1
                if kind == "na" and st == 0:
                    part = bank(b)[:, 0:SEQ]
                    dve.tensor_tensor(part, part, NAB[:, hd, qt, :], ALU.add)
                    dve.drain()
                scores = bank(b, count).rearrange("p (c k) -> p c k", c=count)[:, :, 0:n]
                dve.tensor_reduce(small[:, 8 + b:8 + b + count], scores, AX.X, ALU.max, negate=True)\
                   .then_inc(S["max_ready"], 1)

            def weights(u):
                kind, st, hd, qt = units[u]
                g = u0 + u
                dve.wait_ge(S["exp_done"], g + 1)
                n = TOK - st * SEQ
                b = 12 + 2 * (u % 2)
                r = small[:, 16:18]
                dve.drain()
                dve.reciprocal(r[:, 0:2 if kind == "diff" else 1], small[:, b:b + (2 if kind == "diff" else 1)])
                dve.drain()
                e = EXPO[:, u % 2]
                if kind == "diff":
                    dve.tensor_tensor(small[:, 18:19], r[:, 1:2], neg_lam, ALU.mult)
                    dve.tensor_scalar(e[:, 0, 0:n], e[:, 0, 0:n], r[:, 0:1], None, ALU.mult)
                    dve.drain()
                    dve.scalar_tensor_tensor(e[:, 0, 0:n], e[:, 1, 0:n], small[:, 18:19], e[:, 0, 0:n],
                                             ALU.mult, ALU.add).then_inc(S["weights_ready"], 1)
                else:
                    dve.tensor_scalar(e[:, 0, 0:n], e[:, 0, 0:n], r[:, 0:1], None, ALU.mult)\
                       .then_inc(S["weights_ready"], 1)

            def copy_o(u):
                kind, st, hd, qt = units[u]
                g = u0 + u
                dve.wait_ge(S["o_ready"], g + 1)
                p = (hd % 2) * 64
                tok = st * SEQ + qt * 128
                dve.tensor_copy(y[p:p + 64, (2 if kind == "diff" else 4) + hd // 2, tok:tok + 128],
                                bank(6)[p:p + 64, 0:128]).then_inc(S["o_copied"], 1)

            n = len(units)
            for u in range(n + 3):
                if u < n:
                    maxima(u)
                if 1 <= u <= n:
                    weights(u - 1)
                if u >= 3:
                    copy_o(u - 3)
            dve.drain()

        def units_of(li):
            out = []
            for st in range(2 if li < DEPTH - 1 else 1):
                out += [(kind, st, hd, qt) for kind in ("diff", "na") for hd in range(4) for qt in range(2)]
            return out

        UNITS = [units_of(li) for li in range(DEPTH)]
        U0 = [0, len(UNITS[0])]

        def pe_mixers1(pe, li):
            if li == 0:
                pe.wait_ge(S["loaded_c1"], 32)
            pe.wait_ge(S["bank_free"], sched[f"1in{li}"][1] + 2 * IN1_CHUNKS)
            for half in range(2):
                pe.wait_ge(S["qk_sq"], 2 * li + half + 1)
                for i in range(4):
                    ins = pe.matmul(bank(4 * half + i), c1("blk32" if half == 0 else "blk64"),
                                    SCR[:, (4 * half + i) * 512:(4 * half + i + 1) * 512], start=True, stop=True)
                ins.then_inc(S["qk_sum"], 1)
            pe.wait_ge(S["qk_normed"], li + 1)
            for i in range(4):
                ins = pe.matmul(bank(i)[:, 0:SEQ], c1("rope"), P[:, 2 + i, 0:SEQ], start=True, stop=True)
            ins.then_inc(S["rot_ready"], 1)
            dft_n = c1("dft_n", 1024).rearrange("p (t c) -> p t c", t=2)
            for s in range(2):
                for m in range(2):
                    for tt in range(2):
                        ins = pe.matmul(bank(4 + 2 * m + s), P[:, s, tt * 256 + m * 128:tt * 256 + m * 128 + 128],
                                        dft_n[:, tt, :], start=tt == 0, stop=tt == 1)
            ins.then_inc(S["f_cols"], 1)
            pe.wait_ge(S["f_copied"], li + 1)
            u = SCR[:, 0:2048].rearrange("p (m s c) -> p m s c", m=2, s=2)
            for m in range(2):
                for s in range(2):
                    o = bank(4 + m)[:, s * SEQ:(s + 1) * SEQ]
                    pe.matmul(o, c1("dft_c"), u[:, m, s, 0:256], start=True, stop=False)
                    ins = pe.matmul(o, c1("dft_s"), u[:, m, s, 256:512], start=False, stop=True)
            ins.then_inc(S["f_rows"], 1)
            pe.wait_ge(S["gm_ready"], li + 1)
            ws = d1(f"ws{li}", 512).rearrange("p (g q) -> p g q", g=4)
            for g in range(4):
                for s in range(2):
                    for tt in range(2):
                        p = (g % 2) * 64
                        o = bank(6 + g // 2)[p:p + 64, (2 * s + tt) * 128:(2 * s + tt + 1) * 128]
                        ins = pe.matmul(o, P[:, 16 + s, tt * 256 + g * 64:tt * 256 + g * 64 + 64], ws[:, g, :],
                                        start=True, stop=True)
            ins.then_inc(S["gm_prod"], 1)
            pe.wait_ge(S["qk_ready"], li + 1)
            pe_attention(pe, li, UNITS[li], U0[li])
            pe.wait_ge(S["sub_sq"], li + 1)
            for i in range(2):
                ins = pe.matmul(bank(4 + i), c1("blk64"), SCR[:, i * 512:(i + 1) * 512], start=True, stop=True)
            ins.then_inc(S["sub_sum"], 1)
            pe.wait_ge(S["y_ready"], li + 1)

        def act_rsqrt(act, dst, src, scale):
            act.activation(dst, src, ACT.Ln, bias=eps, scale=scale)
            act.drain()
            return act.activation(dst, dst, ACT.Exp, scale=-0.5)

        def act_mixers1(act, li):
            n0, r0 = sched[f"1in{li}"]
            for rho in range(18):
                act.wait_ge(S["products"], 2 * n0 + rho + 1)
                tok = in1_tokens(li, rho // 2)
                act.copy(P[:, rho, 0:tok], bank(rho % 4)[:, 0:tok]).then_inc(S["bank_free"], 1)
            for half in range(2):
                act.wait_ge(S["qk_sum"], 2 * li + half + 1)
                act_rsqrt(act, SCR[:, half * 2048:(half + 1) * 2048], bank(4 * half, 4),
                          1.0 / (DIFF_QK if half == 0 else HEAD)).then_inc(S["qk_rinv"], 1)
            act.wait_ge(S["g_in"], li + 1)
            act.activation(EXPO_FLAT, EXPO_FLAT, ACT.Tanh, scale=math.sqrt(2.0 / math.pi))\
               .then_inc(S["g_tanh"], 1)
            act.wait_ge(S["lam_in"], li + 1)
            act.activation(small[:, 2:4], small[:, 2:4], ACT.Exp).then_inc(S["lam_exp"], 1)
            act.wait_ge(S["f_cols"], li + 1)
            act.wait_ge(S["qk_normed"], li + 1)
            act.copy(SCR[:, 0:2048], bank(4, 4)).then_inc(S["f_copied"], 1)
            act.wait_ge(S["f_rows"], li + 1)
            act.copy(y[:, 0:2, :], bank(4, 2).rearrange("p (m c) -> p m c", m=2))
            act.wait_ge(S["gm_sq"], li + 1)
            act_rsqrt(act, small[:, 32:48], small[:, 32:48], 1.0 / HEAD).then_inc(S["gm_rinv"], 1)
            act_attention(act, li, UNITS[li], U0[li])
            act.wait_ge(S["sub_sum"], li + 1)
            act_rsqrt(act, SCR[:, 0:1024], bank(4, 2), 1.0 / HEAD).then_inc(S["sub_rinv"], 1)

        EXPO_FLAT = area(17408, 2048)

        def dve_mixers1(dve, li):
            lam_init = 0.8 - 0.6 * math.exp(-0.3 * li)
            n0, r0 = sched[f"1in{li}"]
            dve.drain()
            for i, width in ((0, DIFF_QK), (4, HEAD)):
                dve.tensor_scalar(small[:, 20 + i:22 + i], v(f"qk{li}", 2, i), width ** -0.5, None, ALU.mult)
                dve.tensor_copy(small[:, 22 + i:24 + i], v(f"qk{li}", 2, i + 2))
            if li == 0:
                dve.wait_ge(S["loaded_c1"], 32)
            lam = d1(f"lam{li}", 128).rearrange("p (a b c) -> p a b c", a=2, b=2)
            prod = rinv[:, 0:64].rearrange("p (a c) -> p a c", a=2)
            dve.tensor_tensor(prod, lam[:, :, 0, :], lam[:, :, 1, :], ALU.mult)
            dve.drain()
            dve.tensor_reduce(small[:, 2:4], prod, AX.X, ALU.add).then_inc(S["lam_in"], 1)
            dve.wait_ge(S["loaded_nab"], 256 * (li + 1))
            nab = area(20480, 2048).rearrange("p (n c) -> p n c", c=GRID_W)
            dve.tensor_tensor(nab, nab, spread(c1("namask", 64), 32, 1), ALU.add)
            for half, (first, count) in enumerate(((2, 4), (8, 4))):
                dve.wait_ge(S["bank_free"], r0 + first + count)
                part = P[:, first:first + count, :]
                dve.tensor_tensor(SCR[:, half * 2048:(half + 1) * 2048].rearrange("p (s c) -> p s c", s=4),
                                  part, part, ALU.mult).then_inc(S["qk_sq"], 1)
            dve.wait_ge(S["bank_free"], r0 + 18)
            uv = area(14 * 512, 2048)
            gt = EXPO_FLAT
            dve.drain()
            dve.tensor_tensor(gt, uv, uv, ALU.mult)
            dve.drain()
            dve.tensor_scalar(gt, gt, 0.044715, 1.0, ALU.mult, ALU.add)
            dve.drain()
            dve.tensor_tensor(gt, gt, uv, ALU.mult).then_inc(S["g_in"], 1)
            for half, first in enumerate((2, 8)):
                dve.wait_ge(S["qk_rinv"], 2 * li + half + 1)
                for i in range(4):
                    dve.scalar_tensor_tensor(P[:, first + i, :], P[:, first + i, :],
                                             small[:, 20 + 4 * half + i:21 + 4 * half + i],
                                             SCR[:, (4 * half + i) * 512:(4 * half + i + 1) * 512], ALU.mult, ALU.mult)
            dve.drain().then_inc(S["qk_normed"], 1)
            dve.wait_ge(S["g_tanh"], li + 1)
            dve.tensor_scalar(gt, gt, 0.5, 0.5, ALU.mult, ALU.add)
            dve.drain()
            dve.tensor_tensor(uv, uv, gt, ALU.mult)
            dve.drain()
            vpart = area(16 * 512, 1024)
            vsq = EXPO_FLAT[:, 0:1024]
            dve.drain()
            dve.tensor_tensor(vsq, vpart, vpart, ALU.mult)
            dve.drain()
            dve.tensor_reduce(small[:, 32:48], vsq.rearrange("p (a c) -> p a c", c=HEAD), AX.X, ALU.add)\
               .then_inc(S["gm_sq"], 1)
            dve.wait_ge(S["rot_ready"], li + 1)
            rot = bank(0, 4).rearrange("p (s c) -> p s c", s=4)[:, :, 0:SEQ]
            tmp = EXPO_FLAT[:, 0:1024].rearrange("p (s c) -> p s c", s=4)
            qk = P[:, 2:6, 0:SEQ]
            dve.drain()
            dve.tensor_tensor(tmp, rot, spread(c1("sin", 256), 4, 1), ALU.mult)
            dve.tensor_tensor(qk, qk, spread(c1("cos", 256), 4, 1), ALU.mult)
            dve.drain()
            dve.tensor_tensor(qk, qk, tmp, ALU.add)
            dve.drain()
            dve.wait_ge(S["lam_exp"], li + 1)
            dve.tensor_tensor(small[:, 4:5], small[:, 3:4], small[:, 2:3], ALU.subtract)
            dve.drain()
            dve.tensor_scalar(small[:, 4:5], small[:, 4:5], lam_init, None, ALU.subtract)
            dve.drain()
            dve.wait_ge(S["gm_rinv"], li + 1)
            v3 = vpart.rearrange("p (a c) -> p a c", c=HEAD)
            dve.tensor_tensor(v3, v3, spread(small[:, 32:48], HEAD, 2), ALU.mult).then_inc(S["gm_ready"], 1)
            dve.wait_ge(S["gm_prod"], li + 1)
            gb = d1(f"gb{li}", 256).rearrange("p (g q) -> p g q", g=2)
            for g in range(2):
                o = y[:, 6 + g, :].rearrange("p (a q) -> p a q", a=4)
                dve.scalar_tensor_tensor(o, bank(6 + g).rearrange("p (a q) -> p a q", a=4), v(f"gmlp_norm{li}", 1, g),
                                         spread(gb[:, g, :], 4, 1), ALU.mult, ALU.add)
            dve.drain()
            dve.tensor_tensor(y[:, 6:8, :], y[:, 6:8, :], P[:, 14:16, :], ALU.mult)
            dve.drain().then_inc(S["qk_ready"], 1)
            dve_attention(dve, li, UNITS[li], U0[li])
            o = y[:, 2:4, :]
            dve.tensor_tensor(SCR[:, 0:1024].rearrange("p (a c) -> p a c", a=2), o, o, ALU.mult)\
               .then_inc(S["sub_sq"], 1)
            dve.tensor_scalar(small[:, 19:20], v(f"subln{li}"), 1.0 - lam_init, None, ALU.mult)
            dve.wait_ge(S["sub_rinv"], li + 1)
            dve.drain()
            dve.scalar_tensor_tensor(o, o, small[:, 19:20], SCR[:, 0:1024].rearrange("p (a c) -> p a c", a=2),
                                     ALU.mult, ALU.mult)
            dve.drain().then_inc(S["y_ready"], 1)

        def pe_ffn1(pe, li):
            tok = TOK if li < DEPTH - 1 else SEQ
            n0, r0 = sched[f"1up{li}"]
            pe.wait_ge(S["h_ready"], KT * (2 * li + 2))

            def up(i, c):
                arrived(pe, n0 + c, i)
                for half in range(2):
                    rho = 2 * c + half
                    free = r0 + rho - 3
                    pe.wait_ge(S["bank_free"], free if i is None else 2 * RING * i + free)
                    k_products(pe, bank(rho % 4)[:, 0:tok],
                               lambda k: w[:, (n0 + c) % RING, k, half * 128:(half + 1) * 128],
                               lambda k: h[:, k, 0:tok])

            with pe.Fori(0, UP_CHUNKS // RING) as i:
                for c in range(RING):
                    up(i, c)
            for c in range(UP_CHUNKS // RING * RING, UP_CHUNKS):
                up(None, c)
            pe.wait_ge(S["act_ready"], PAIRS * (li + 1) + 1)
            pe_residual(pe, f"1down{li}", act1, FT_GROUPS, FT, tok)

        def act_ffn1(act, li):
            tok = TOK if li < DEPTH - 1 else SEQ
            n0, r0 = sched[f"1up{li}"]
            with act.Fori(0, PAIRS) as j:
                for q in range(4):
                    act.wait_ge(S["products"], 4 * j + (2 * n0 + q + 1))
                    if q == 0:
                        act.wait_ge(S["act_ready"], j + (PAIRS * li + 1))
                    col = VEC[f"conv{li}"] + 4 * q
                    act.activation(Z[:, q, 0:tok], bank(q)[:, 0:tok], ACT.Identity,
                                   scale=vec[:, bass.ds(16 * j + (col + 1), 1)],
                                   bias=vec[:, bass.ds(16 * j + (col + 3), 1)]).then_inc(S["z_init"], 1)
                act.wait_ge(S["conv_done"], j + (PAIRS * li + 1))
                act.activation(ZE[:, :, 0:tok], Z[:, 0:2, 0:tok], ACT.Tanh, scale=0.5).then_inc(S["sig_tanh"], 1)

        def dve_ffn1(dve, li):
            streams = 2 if li < DEPTH - 1 else 1
            tok = streams * SEQ
            with dve.Fori(0, PAIRS) as j:
                for q in range(4):
                    dve.wait_ge(S["z_init"], 4 * j + (4 * PAIRS * li + q + 1))
                    z = Z[:, q, 0:tok].rearrange("p (s c) -> p s c", s=streams)
                    z0 = bank(q)[:, 0:tok].rearrange("p (s c) -> p s c", s=streams)
                    col = VEC[f"conv{li}"] + 4 * q
                    dve.scalar_tensor_tensor(z[:, :, 1:SEQ], z0[:, :, 0:SEQ - 1], vec[:, bass.ds(16 * j + col, 1)],
                                             z[:, :, 1:SEQ], ALU.mult, ALU.add)
                    dve.drain()
                    dve.scalar_tensor_tensor(z[:, :, 0:SEQ - 1], z0[:, :, 1:SEQ], vec[:, bass.ds(16 * j + (col + 2), 1)],
                                             z[:, :, 0:SEQ - 1], ALU.mult, ALU.add).then_inc(S["bank_free"], 1)
                dve.drain().then_inc(S["conv_done"], 1)
                dve.wait_ge(S["sig_tanh"], j + (PAIRS * li + 1))
                e = ZE[:, :, 0:tok]
                dve.tensor_tensor(Z[:, 2:4, 0:tok], Z[:, 0:2, 0:tok], Z[:, 2:4, 0:tok], ALU.mult)
                dve.tensor_scalar(e, e, 0.5, 0.5, ALU.mult, ALU.add)
                dve.drain()
                dve.tensor_tensor(act1[:, bass.ds(2 * j, 2), 0:tok], e, Z[:, 2:4, 0:tok], ALU.mult)\
                   .then_inc(S["act_ready"], 1)
            dve_residual(dve, f"1down{li}", FT_GROUPS, 5, streams)

        def act_norm(act, k, part):
            act.wait_ge(S["n_sum"], k + 1)
            act_rsqrt(act, rinv[:, :], bank(5), 1.0 / D).then_inc(S["n_rinv"], 1)
            for kt in range(KT):
                act.wait_ge(S["n_normed"], KT * k + kt + 1)
                for s in range(2):
                    hp = h[:, kt, s * SEQ:(s + 1) * SEQ]
                    ins = act.activation(hp, hp, ACT.Identity, scale=a_mul[:, part, kt, s:s + 1],
                                         bias=mod[:, 3 * part * KT + kt, s:s + 1])
                ins.then_inc(S["h_ready"], 1)

        def dve_norm(dve, k):
            dve.drain()
            dve.tensor_tensor(h_sb[:, :], x_sb[:, :], x_sb[:, :], ALU.mult).then_inc(S["n_sq"], 1)
            dve.wait_ge(S["n_rinv"], k + 1)
            for kt in range(KT):
                dve.tensor_tensor(h[:, kt, :], x[:, kt, :], rinv[:, :], ALU.mult).then_inc(S["n_normed"], 1)

        def dve_mods(dve, k, bias, gains):
            if k in (1, 2):
                dve.wait_ge(S["next_turned"], ADA_CHUNKS * k)
                turned = bank(7)[:, 256:352]
            else:
                dve.wait_ge(S["ada_turned"], ADA_GROUPS * (1 + k // 3))
                turned = bank(6)[:, 0:96]
            dve.tensor_tensor(mod, turned.rearrange("p (m s) -> p m s", s=2), spread(v(bias, 48), 2, 2), ALU.add)
            dve.drain()
            for i, g in enumerate(gains):
                dve.tensor_scalar(a_mul[:, i, :, :], mod[:, (1 + 3 * i) * KT:(2 + 3 * i) * KT, :], 1.0, None, ALU.add)
                dve.drain()
                dve.tensor_tensor(a_mul[:, i, :, :], a_mul[:, i, :, :], spread(v(g, KT), 2, 2), ALU.mult)
            dve.drain().then_inc(S["mods_ready"], 1)

        B.update(locals())
        block = ctx.enter_context(nc.Block())

        @block.sync
        def _(sp):
            for n in range(RING):
                sp.dma_start(ring[:, n * CHUNK:(n + 1) * CHUNK], t["stream"][n]).then_inc(slot_sem[n], 16)

            def load(i, n):
                used = 2 * (n - RING + 1)
                sp.wait_ge(S["products"], used if i is None else 2 * RING * i + used)
                slot = n % RING
                src = t["stream"][n] if i is None else t["stream"][bass.ds(RING * i + n, 1)].rearrange("a p c -> (a p) c")
                sp.dma_start(ring[:, slot * CHUNK:(slot + 1) * CHUNK], src).then_inc(slot_sem[slot], 16)

            with sp.Fori(0, total_chunks // RING - 1) as i:
                for c in range(RING):
                    load(i, RING + c)
            for n in range(total_chunks // RING * RING, total_chunks):
                load(None, n)
            sp.wait_ge(S["stored"], 16)

        @block.scalar
        def _(act):
            act.dma_start(vec[:, :], t["vec"]).then_inc(S["loaded_vec"], 16)
            act.dma_start(ident[:, :], t["ident"]).then_inc(S["loaded_vec"], 16)
            act.dma_start(ones[:, :], t["ones"]).then_inc(S["loaded_vec"], 16)
            act.dma_start(x_sb[:, :], t["x"]).then_inc(S["loaded_x"], 16)
            act.dma_start(arena[:, CONST1:CONST1 + C1["end"]], t["c1"]).then_inc(S["loaded_c1"], 16)
            act.dma_start(arena[:, DATA1:DATA1 + D1["end"]], t["d1"]).then_inc(S["loaded_c1"], 16)

            def load_nab(li):
                rpb = t["rpb"]
                for hd in range(4):
                    for qt in range(2):
                        for r in range(2):
                            row = 7 - (2 * qt + r)
                            off = ((li * 4 + hd) * GRID_W * RPB_H + row) * RPB_W + 15
                            src = bass.AP(tensor=rpb.tensor, offset=off,
                                          ap=[[RPB_H * RPB_W - 1, GRID_W], [RPB_W, 4], [1, GRID_W]])
                            act.dma_start(NAB[r * 64:(r + 1) * 64, hd, qt, :].rearrange("p (a c) -> p a c", a=4), src)\
                               .then_inc(S["loaded_nab"], 16)

            act.wait_ge(S["loaded_vec"], 48)
            act.activation(silu_c[:, :], v("c", 4 * KT), ACT.Tanh, scale=0.5).then_inc(S["silu_tanh"], 1)
            load_nab(0)
            for li in range(DEPTH):
                if li == 0:
                    act_ada(act, "1ada0", 0)
                act.wait_ge(S["mods_ready"], li + 1)
                if li > 0:
                    load_nab(li)
                act_norm(act, 2 * li, 0)
                act_mixers1(act, li)
                act_norm(act, 2 * li + 1, 1)
                act_ffn1(act, li)
            if second:
                second.act(act)

        @block.vector
        def _(dve):
            dve.memset(eps, EPS)
            dve.drain().then_inc(S["act_ready"], 1)
            dve.wait_ge(S["silu_tanh"], 1)
            dve.tensor_scalar(silu_c[:, :], silu_c[:, :], 0.5, 0.5, ALU.mult, ALU.add)
            dve.drain()
            dve.tensor_tensor(silu_c[:, :], silu_c[:, :], v("c", 4 * KT), ALU.mult).then_inc(S["silu_ready"], 1)
            dve.wait_ge(S["loaded_x"], 16)
            for li in range(DEPTH):
                streams = 2 if li < DEPTH - 1 else 1
                dve_mods(dve, li, f"b_ada{li}", (f"g_mix{li}", f"g_ffn{li}"))
                dve_norm(dve, 2 * li)
                dve_mixers1(dve, li)
                dve_residual(dve, f"1out{li}", 1, 2, streams)
                dve_norm(dve, 2 * li + 1)
                dve_ffn1(dve, li)
            if second:
                second.dve(dve)
            else:
                dve.drain().then_inc(S["x_done"], 1)

        @block.tensor
        def _(pe):
            pe.wait_ge(S["loaded_vec"], 48)
            for li in range(DEPTH):
                tok = TOK if li < DEPTH - 1 else SEQ
                if li == 0:
                    pe_ada(pe, "1ada0", 0, 0)
                pe_norm(pe, 2 * li)
                pe_in1(pe, li)
                pe_mixers1(pe, li)
                pe_residual(pe, f"1out{li}", y, 1, KT, tok)
                pe_norm(pe, 2 * li + 1)
                pe_ffn1(pe, li)
            if second:
                second.pe(pe)

        @block.gpsimd
        def _(pool):
            if second:
                second.pool(pool)
            pool.wait_ge(S["x_done"], 1)
            pool.dma_start(out.rearrange("p (k c) -> p k c", k=KT), x[:, :, 0:SEQ]).then_inc(S["stored"], 16)


QKV_CHUNKS = 16
Z_CHUNKS = 8
DN_HEADS = 16
UP2_CHUNKS = D_FF2 // CHUNK_COLS
GLA_CHUNKS = 12
GLA_DK = 128
C2 = _offsets([("tri0", 128), ("tri1", 128), ("lev0", LEVELS * 128), ("lev1", LEVELS * 128)])
ORDER = ((2, 3, 0, 1), (3, 2, 1, 0))
LAST = (DELTA_C - 1, 0)


def plan_second(plan):
    plan("2qkv", QKV_CHUNKS, 2 * QKV_CHUNKS)
    plan("2z", Z_CHUNKS, 2 * Z_CHUNKS)
    plan("2out0", OUT_CHUNKS * 2, KT)
    plan("2up0", UP2_CHUNKS, 2 * UP2_CHUNKS)
    plan("2down0", OUT_CHUNKS * 4, KT)
    if LAYERS2 == 1:
        return
    plan("2ada1", ADA_CHUNKS, 0)
    plan("2gla", GLA_CHUNKS, 2 * GLA_CHUNKS)
    plan("2out1", OUT_CHUNKS, KT)
    plan("2up1", UP2_CHUNKS, 2 * UP2_CHUNKS)
    plan("2down1", OUT_CHUNKS * 4, KT)


class SecondBlock:

    def __init__(self, b):
        self.b = b
        self.norm1, self.mods1 = 7, 3
        self.c2 = b["sb"]("c2", C2["end"])
        self.gates = b["sb"]("gates", 6 * 128)
        self.kst = b["sb"]("kst", 1024)
        self.S2 = b["sems"]("""loaded_c2 arena_free ab_psum ab_tanh ab_exp ab_ln ab_in g_ready gc_psum gc_ready
            l_sq l_sum l_rinv l_done v_psum_t v_copied kst_ready kst_free
            gbc0 gbc1 pre0 pre1 dec_in0 dec_in1 dec0 dec1 masked0 masked1 d_ready0 d_ready1 dt_psum0 dt_psum1
            dt_ready0 dt_ready1 yp0 yp1 yr0 yr1 pp0 pp1 lev0 lev1 ks0 ks1 r0 r1 vn0 vn1 vr0 vr1 op0 op1
            done0 done1 fac0 fac1
            taps tapped tanh5 qkv_ready o_normed z_tanh z_ready relu2 sq2
            low_psum low_ready lg_psum lg_in lg_exp lg_ln gk_ready b_psum b_copied kt_arg kt_exp kt_fm kt_psum kt_tok
            w_arg w_exp w_q w_k a_psum a_read at_ready gs_ready o2_psum s_done gate_tanh gate_done
            or_sq or_sum or_rinv oy_ready eb_ready""")

    def views(self):
        area = self.b["area"]
        self.q = area(0, 4096, s=8)
        self.k = area(4096, 4096, s=8)
        self.o = area(8192, 8192, s=16)
        self.vtok = area(16384, 8192, t=4, h=DN_HEADS)
        self.buf = [area(24576 + 512 * n, 512) for n in range(8)] + \
                   [self.b["h_sb"][:, 512 * n:512 * (n + 1)] for n in range(8)]
        g = self.gates
        self.g_, self.beta, self.gcum, self.begn, self.t1, self.t2 = (
            g[:, 128 * n:128 * (n + 1)].rearrange("p (t h) -> p t h", t=4) for n in range(6))

    def tri(self, d):
        return self.c2[:, C2[f"tri{d}"]:C2[f"tri{d}"] + 128]

    def lev(self, d, level):
        at = C2[f"lev{d}"] + 128 * level
        return self.c2[:, at:at + 128]

    def pe_tiles(self, pe, name, chunks, tok):
        b = self.b
        n0, r0 = b["sched"][name]
        with pe.Fori(0, chunks // RING) as i:
            for c in range(RING):
                b["arrived"](pe, n0 + c, i)
                for half in range(2):
                    rho = 2 * c + half
                    pe.wait_ge(b["S"]["bank_free"], 2 * RING * i + (r0 + rho - 3))
                    b["k_products"](pe, b["bank"](rho % 4)[:, 0:tok],
                                    lambda k: b["w"][:, (n0 + c) % RING, k, half * 128:(half + 1) * 128],
                                    lambda k: b["h"][:, k, 0:tok])

    def pe_norms(self, pe, inst, batches):
        for g in range(batches):
            pe.wait_ge(self.S2["l_sq"], inst + g + 1)
            for i in range(4):
                ins = pe.matmul(self.b["bank"](4 + i), self.b["ones"][:, :], self.buf[i], start=True, stop=True)
            ins.then_inc(self.S2["l_sum"], 1)

    def act_norms(self, act, inst, batches, scale):
        for g in range(batches):
            act.wait_ge(self.S2["l_sum"], inst + g + 1)
            self.b["act_rsqrt"](act, self.b["area"](26624, 2048), self.b["bank"](4, 4), scale)\
                .then_inc(self.S2["l_rinv"], 1)

    def dve_norms(self, dve, inst, batches, src, scalar):
        for g in range(batches):
            part = src[:, 2048 * g:2048 * (g + 1)]
            dve.drain()
            dve.tensor_tensor(self.b["area"](24576, 2048), part, part, ALU.mult).then_inc(self.S2["l_sq"], 1)
            dve.wait_ge(self.S2["l_rinv"], inst + g + 1)
            dve.scalar_tensor_tensor(part, part, scalar(g), self.b["area"](26624, 2048), ALU.mult, ALU.mult)
        dve.drain()

    def pe_delta(self, pe):
        b, S, T = self.b, self.b["S"], self.S2
        bank, h = b["bank"], b["h"]
        pe.wait_ge(S["h_ready"], KT * 5)
        self.pe_tiles(pe, "2qkv", QKV_CHUNKS, TOK)
        pe.wait_ge(T["loaded_c2"], 80)
        wab = self.kst[:, 0:512].rearrange("p (k c) -> p k c", k=KT)
        for tt in range(4):
            for k in range(KT):
                ins = pe.matmul(bank(4)[:, tt * 64:(tt + 1) * 64], h[:, k, tt * 128:(tt + 1) * 128], wab[:, k, :],
                                start=k == 0, stop=k == KT - 1)
        ins.then_inc(T["ab_psum"], 1)
        pe.wait_ge(T["g_ready"], 1)
        for d in range(2):
            for tt in range(4):
                ins = pe.matmul(bank(5)[:, tt * 32 + d * 16:tt * 32 + d * 16 + 16], self.tri(d),
                                self.g_[:, tt, d * 16:(d + 1) * 16], start=True, stop=True)
        ins.then_inc(T["gc_psum"], 1)
        pe.wait_ge(T["gc_ready"], 1)
        self.pe_norms(pe, 0, 4)
        for hv in range(DN_HEADS):
            if hv >= 4:
                pe.wait_ge(T["v_copied"], hv - 3)
            for tt in range(4):
                ins = pe.transpose(bank(hv % 4)[:, tt * 128:(tt + 1) * 128], self.o[:, hv, tt * 128:(tt + 1) * 128],
                                   b["ident"][:, :])
            ins.then_inc(T["v_psum_t"], 1)
        pe.wait_ge(T["l_done"], 1)
        pe.wait_ge(T["v_copied"], DN_HEADS)
        with pe.Fori(0, 4) as i:
            pe.wait_ge(T["kst_ready"], i + 1)
            for c in range(4):
                self.pe_delta_step(pe, i, c)

    def pe_delta_step(self, pe, i, c):
        b, T, bank, ident = self.b, self.S2, self.b["bank"], self.b["ident"]
        kst = self.kst[:, :].rearrange("p (k t) -> p k t", k=2)

        def each(out, lhs, rhs, **flags):
            for n in range(4):
                ins = pe.matmul(out[:, n * 128:(n + 1) * 128], lhs(n), rhs(n), **(flags or dict(start=True, stop=True)))
            return ins

        def part(a):
            return lambda n: a[:, n * 128:(n + 1) * 128]

        for d in range(2):
            S_, M, AT, QE, KTL, D_, DT, Y = self.buf[8 * d:8 * d + 8]
            tok = ORDER[d][c] * 128
            at = 4 * i + c
            pe.wait_ge(T[f"gbc{d}"], at + 1)
            each(bank(4 * d), part(D_), lambda n: self.tri(d))
            pe.wait_ge(T[f"done{d}"], at + 1)
            for n in range(2):
                key = kst[:, n, tok:tok + 128]
                pe.matmul(bank(4 * d + 1)[:, n * 128:(n + 1) * 128], key, key, start=True, stop=True)
                pe.matmul(bank(4 * d + 1)[:, (2 + n) * 128:(3 + n) * 128], key,
                          b["area"](0, 4096)[:, bass.ds(1024 * i + (512 * n + tok), 128)], start=True, stop=True)
                ins = pe.transpose(bank(4 * d + 3)[:, n * 128:(n + 1) * 128], key, ident[:, :])
            ins.then_inc(T[f"pre{d}"], 1)
        for d in range(2):
            S_, M, AT, QE, KTL, D_, DT, Y = self.buf[8 * d:8 * d + 8]
            pe.wait_ge(T[f"d_ready{d}"], 4 * i + (c + 1))
            for n in range(4):
                ins = pe.transpose(bank(4 * d)[:, n * 128:(n + 1) * 128], part(D_)(n), ident[:, :])
            ins.then_inc(T[f"dt_psum{d}"], 1)
        for level in range(1, LEVELS):
            last = level == LEVELS - 1
            for d in range(2):
                S_, M, AT, QE, KTL, D_, DT, Y = self.buf[8 * d:8 * d + 8]
                if level == 1:
                    pe.wait_ge(T[f"dt_ready{d}"], 4 * i + (c + 1))
                else:
                    pe.wait_ge(T[f"lev{d}"], 24 * i + (6 * c + level - 1))
                each(bank(4 * d + 2), part(M), part(DT)).then_inc(T[f"yp{d}"], 1)
            for d in range(2):
                S_, M, AT, QE, KTL, D_, DT, Y = self.buf[8 * d:8 * d + 8]
                pe.wait_ge(T[f"yr{d}"], 24 * i + (6 * c + level))
                ins = each(bank(4 * d), part(D_), part(Y))
                if not last:
                    ins = each(bank(4 * d + 1), part(Y), part(D_))
                ins.then_inc(T[f"pp{d}"], 1)
        for d in range(2):
            S_, M, AT, QE, KTL, D_, DT, Y = self.buf[8 * d:8 * d + 8]
            tok = ORDER[d][c] * 128
            each(bank(4 * d + 2), lambda n: kst[:, n // 2, tok:tok + 128], part(S_)).then_inc(T[f"ks{d}"], 1)
        for d in range(2):
            S_, M, AT, QE, KTL, D_, DT, Y = self.buf[8 * d:8 * d + 8]
            pe.wait_ge(T[f"r{d}"], 4 * i + (c + 1))
            each(bank(4 * d), part(DT), part(D_)).then_inc(T[f"vn{d}"], 1)
        for d in range(2):
            S_, M, AT, QE, KTL, D_, DT, Y = self.buf[8 * d:8 * d + 8]
            pe.wait_ge(T[f"vr{d}"], 4 * i + (c + 1))
            pe.wait_ge(T[f"masked{d}"], 4 * i + (c + 1))
            for n in range(4):
                pe.matmul(bank(4 * d + 1)[:, n * 128:(n + 1) * 128], part(S_)(n), part(QE)(n), start=True, stop=False)
                pe.matmul(bank(4 * d + 1)[:, n * 128:(n + 1) * 128], part(Y)(n), part(AT)(n), start=False, stop=True)
            each(bank(4 * d + 2), part(KTL), part(Y)).then_inc(T[f"op{d}"], 1)

    def act_delta(self, act):
        b, S, T = self.b, self.b["S"], self.S2
        bank = b["bank"]
        n0, r0 = b["sched"]["2qkv"]
        Z = b["area"](24576, 2048, q=4)
        ZE = b["area"](26624, 2048)
        with act.Fori(0, QKV_CHUNKS // 2) as j:
            for q in range(4):
                act.wait_ge(S["products"], 4 * j + (2 * n0 + q + 1))
                if q == 0:
                    act.wait_ge(T["qkv_ready"], j + 1)
                act.activation(Z[:, q, :], bank(q), ACT.Copy,
                               scale=b["vec"][:, bass.ds(20 * j + (VEC["dn_conv"] + 5 * q + 2), 1)])\
                   .then_inc(T["taps"], 1)
            act.wait_ge(T["tapped"], j + 1)
            act.activation(ZE, b["area"](24576, 2048), ACT.Tanh, scale=0.5).then_inc(T["tanh5"], 1)
        act.wait_ge(T["ab_psum"], 1)
        act.wait_ge(T["ab_in"], 1)
        ab = bank(4)[:, 0:256].rearrange("p (t c) -> p t c", t=4)
        act.activation(self.beta, ab[:, :, 32:64], ACT.Tanh, scale=0.5)
        act.activation(self.t1, self.t1, ACT.Exp)
        act.activation(b["small"][:, 64:96], b["small"][:, 64:96], ACT.Exp)
        act.drain()
        act.activation(self.t1, self.t1, ACT.Ln, bias=1.0)
        act.drain().then_inc(T["ab_ln"], 1)
        act.wait_ge(T["gc_psum"], 1)
        act.copy(self.gcum, bank(5)[:, 0:128].rearrange("p (t c) -> p t c", t=4))
        act.drain()
        act.activation(self.begn, self.gcum, ACT.Exp)
        act.drain().then_inc(T["gc_ready"], 1)
        self.act_norms(act, 0, 4, 1.0)
        for hv in range(DN_HEADS):
            act.wait_ge(T["v_psum_t"], hv + 1)
            act.copy(self.vtok[:, :, hv, :], bank(hv % 4).rearrange("p (t c) -> p t c", t=4)).then_inc(T["v_copied"], 1)
        with act.Fori(0, 4) as i:
            for c in range(4):
                for d in range(2):
                    S_, M, AT, QE, KTL, D_, DT, Y = self.buf[8 * d:8 * d + 8]
                    act.wait_ge(T[f"dec_in{d}"], 4 * i + (c + 1))
                    act.activation(M, M, ACT.Exp, scale=-1.0)
                    act.activation(AT, AT, ACT.Exp)
                    act.activation(QE, bank(4 * d), ACT.Exp).then_inc(T[f"dec{d}"], 1)
                for d in range(2):
                    DT = self.buf[8 * d + 6]
                    act.wait_ge(T[f"dt_psum{d}"], 4 * i + (c + 1))
                    act.copy(DT, bank(4 * d)).then_inc(T[f"dt_ready{d}"], 1)
                for d in range(2):
                    Y = self.buf[8 * d + 7]
                    act.wait_ge(T[f"vn{d}"], 4 * i + (c + 1))
                    act.copy(Y, bank(4 * d)).then_inc(T[f"vr{d}"], 1)
        self.act_norms(act, 4, 4, 1.0 / 128)
        b["act_norm"](act, 5, 0)
        n0, r0 = b["sched"]["2z"]
        with act.Fori(0, Z_CHUNKS // 2) as j:
            for q in range(4):
                act.wait_ge(S["products"], 4 * j + (2 * n0 + q + 1))
                if q == 0:
                    act.wait_ge(T["z_ready"], j + 1)
                act.activation(Z[:, q, :], bank(q), ACT.Tanh, scale=0.5).then_inc(T["z_tanh"], 1)

    def pool_delta(self, pool):
        T = self.S2
        arena = self.b["arena"]
        pool.wait_ge(T["l_done"], 1)
        with pool.Fori(0, 4) as i:
            for d in range(2):
                pool.wait_ge(T[f"done{d}"], 4 * i + 1)
            pool.tensor_copy(self.kst[:, :], arena[:, bass.ds(1024 * i + 4096, 1024)]).then_inc(T["kst_ready"], 1)
            for d in range(2):
                pool.memset(self.buf[8 * d], 0.0)
            pool.drain()
            for c in range(4):
                for d in range(2):
                    S_, M, AT, QE, KTL, D_, DT, Y = self.buf[8 * d:8 * d + 8]
                    tt = ORDER[d][c]
                    if c > 0:
                        pool.wait_ge(T[f"vn{d}"], 4 * i + c)
                    pool.tensor_copy(D_.rearrange("p (h c) -> p h c", h=4),
                                     self.b["spread"](self.gates[:, bass.ds(4 * i + (32 * tt + 16 * d), 4)], 128, 2))\
                        .then_inc(T[f"gbc{d}"], 1)
                for d in range(2):
                    S_, M, AT, QE, KTL, D_, DT, Y = self.buf[8 * d:8 * d + 8]
                    tok = ORDER[d][c] * 128
                    pool.wait_ge(T[f"fac{d}"], 4 * i + (c + 1))
                    at = AT.rearrange("p (h c) -> p h c", h=4)
                    pool.tensor_tensor(at, at, self.b["spread"](self.tri(d), 4, 1), ALU.mult)
                    for n in range(2):
                        qe = QE[:, n * 256:(n + 1) * 256].rearrange("p (r c) -> p r c", r=2)
                        q = arena[:, bass.ds(1024 * i + (512 * n + tok), 128)]
                        pool.tensor_tensor(qe, qe, self.b["spread"](q, 2, 1), ALU.mult)
                    pool.drain().then_inc(T[f"masked{d}"], 1)

    def dve_delta(self, dve):
        b, S, T = self.b, self.b["S"], self.S2
        bank, spread, small, vec = b["bank"], b["spread"], b["small"], b["vec"]
        Z = b["area"](24576, 2048, q=4)
        Zf, ZE = b["area"](24576, 2048), b["area"](26624, 2048)
        dve.drain().then_inc(T["qkv_ready"], 1)
        with dve.Fori(0, QKV_CHUNKS // 2) as j:
            for q in range(4):
                dve.wait_ge(T["taps"], 4 * j + (q + 1))
                z = Z[:, q, :].rearrange("p (s c) -> p s c", s=2)
                u = bank(q).rearrange("p (s c) -> p s c", s=2)
                for n, shift in enumerate((-2, -1, 1, 2)):
                    tap = vec[:, bass.ds(20 * j + (VEC["dn_conv"] + 5 * q + 2 + shift), 1)]
                    lo, hi = max(0, -shift), SEQ - max(0, shift)
                    ins = dve.scalar_tensor_tensor(z[:, :, lo:hi], u[:, :, lo + shift:hi + shift], tap, z[:, :, lo:hi],
                                                   ALU.mult, ALU.add)
                    if n < 3:
                        dve.drain()
                ins.then_inc(S["bank_free"], 1)
            dve.drain().then_inc(T["tapped"], 1)
            dve.wait_ge(T["tanh5"], j + 1)
            dve.tensor_scalar(ZE, ZE, 0.5, 0.5, ALU.mult, ALU.add)
            dve.drain()
            dve.tensor_tensor(b["arena"][:, bass.ds(2048 * j, 2048)], Zf, ZE, ALU.mult)
            dve.drain().then_inc(T["qkv_ready"], 1)
        dve.wait_ge(T["ab_psum"], 1)
        ab = bank(4)[:, 0:256].rearrange("p (t c) -> p t c", t=4)
        rows = self.gates[:, 640:704]
        t1, t2 = self.t1, self.g_
        dve.tensor_tensor(t2, ab[:, :, 0:32], spread(small[:, 96:128], 4, 1), ALU.add)
        dve.drain()
        dve.scalar_tensor_tensor(t1, t2, -1.0, t2, ALU.mult, ALU.min)
        dve.drain().then_inc(T["ab_in"], 1)
        dve.wait_ge(T["ab_ln"], 1)
        dve.scalar_tensor_tensor(t2, t2, 0.0, t1, ALU.max, ALU.add)
        dve.drain()
        dve.scalar_tensor_tensor(t2, t2, -1.0, spread(small[:, 64:96], 4, 1), ALU.mult, ALU.mult)
        dve.tensor_scalar(self.beta, self.beta, 0.5, 0.5, ALU.mult, ALU.add)
        dve.drain().then_inc(T["g_ready"], 1)
        dve.wait_ge(T["gc_ready"], 1)
        dve.scalar_tensor_tensor(self.begn, self.begn, -1.0, self.beta, ALU.mult, ALU.mult)
        self.dve_norms(dve, 0, 4, b["arena"], lambda g: 128 ** -0.5 if g < 2 else 1.0)
        dve.wait_ge(T["v_copied"], DN_HEADS)
        dve.drain().then_inc(T["l_done"], 1)
        for d in range(2):
            dve.drain().then_inc(T[f"done{d}"], 1)
        with dve.Fori(0, 4) as i:
            for c in range(4):
                self.dve_delta_step(dve, i, c)
        self.dve_norms(dve, 4, 4, b["arena"][:, 8192:16384], lambda g: b["v"]("dn_norm"))
        b["dve_norm"](dve, 5)
        n0, r0 = b["sched"]["2z"]
        dve.drain().then_inc(T["z_ready"], 1)
        with dve.Fori(0, Z_CHUNKS // 2) as j:
            for q in range(4):
                dve.wait_ge(T["z_tanh"], 4 * j + (q + 1))
                dve.tensor_scalar(Z[:, q, :], Z[:, q, :], 0.5, 0.5, ALU.mult, ALU.add)
                dve.drain()
                dve.tensor_tensor(Z[:, q, :], Z[:, q, :], bank(q), ALU.mult).then_inc(S["bank_free"], 1)
            dve.drain()
            o = b["arena"][:, bass.ds(2048 * j + 8192, 2048)]
            dve.tensor_tensor(o, o, Zf, ALU.mult)
            dve.drain().then_inc(T["z_ready"], 1)

    def dve_delta_step(self, dve, i, c):
        b, T = self.b, self.S2
        bank, spread, small = b["bank"], b["spread"], b["small"]

        def heads(a):
            return a.rearrange("p (h c) -> p h c", h=4)

        def pairs(a):
            return a.rearrange("p (k r c) -> p k r c", k=2, r=2)

        def token_scalars(n, d):
            return spread(self.gates[:, bass.ds(4 * i + (128 * n + 32 * ORDER[d][c] + 16 * d), 4)], 128, 2)

        for d in range(2):
            S_, M, AT, QE, KTL, D_, DT, Y = self.buf[8 * d:8 * d + 8]
            dve.wait_ge(T[f"pre{d}"], 4 * i + (c + 1))
            dve.tensor_tensor(heads(AT), heads(bank(4 * d)), token_scalars(2, d), ALU.subtract)
            dve.drain()
            dve.tensor_scalar(M, AT, 0.0, None, ALU.max)
            dve.drain()
            dve.tensor_scalar(AT, AT, 0.0, None, ALU.min)
            dve.drain().then_inc(T[f"dec_in{d}"], 1)
        for d in range(2):
            S_, M, AT, QE, KTL, D_, DT, Y = self.buf[8 * d:8 * d + 8]
            dve.wait_ge(T[f"dec{d}"], 4 * i + (c + 1))
            last = LAST[d]
            kt = bank(4 * d + 3)[:, 0:256].rearrange("p (k c) -> p k c", k=2)
            tail = heads(AT)[:, :, last:last + 1]
            for n in range(2):
                dve.tensor_tensor(heads(KTL)[:, 2 * n:2 * n + 2, :], spread(kt[:, n, :], 2, 1),
                                  tail[:, 2 * n:2 * n + 2, :].to_broadcast([128, 2, 128]), ALU.mult)
            dve.tensor_copy(small[:, 48 + 4 * d:52 + 4 * d], heads(QE)[:, :, last])
            kk = bank(4 * d + 1)[:, 0:256].rearrange("p (k c) -> p k c", k=2)
            kq = bank(4 * d + 1)[:, 256:512].rearrange("p (k c) -> p k c", k=2)
            dve.tensor_tensor(pairs(M), pairs(M), spread(kk, 2, 2), ALU.mult)
            dve.drain()
            dve.tensor_tensor(heads(M), heads(M), token_scalars(1, d), ALU.mult)
            dve.tensor_tensor(pairs(AT), pairs(AT), spread(kq, 2, 2), ALU.mult).then_inc(T[f"fac{d}"], 1)
            dve.drain()
            dve.tensor_tensor(heads(D_), heads(M), spread(self.lev(1 - d, 0), 4, 1), ALU.mult)
            dve.drain()
            dve.scalar_tensor_tensor(heads(D_), heads(D_), -1.0, spread(b["ident"][:, :], 4, 1), ALU.mult, ALU.add)\
               .then_inc(T[f"d_ready{d}"], 1)
        for level in range(1, LEVELS):
            last = level == LEVELS - 1
            for d in range(2):
                S_, M, AT, QE, KTL, D_, DT, Y = self.buf[8 * d:8 * d + 8]
                dve.wait_ge(T[f"yp{d}"], 24 * i + (6 * c + level))
                dve.tensor_tensor(heads(Y), heads(bank(4 * d + 2)), spread(self.lev(d, level), 4, 1), ALU.mult)\
                   .then_inc(T[f"yr{d}"], 1)
            for d in range(2):
                S_, M, AT, QE, KTL, D_, DT, Y = self.buf[8 * d:8 * d + 8]
                dve.wait_ge(T[f"pp{d}"], 24 * i + (6 * c + level))
                dve.tensor_tensor(DT, DT, bank(4 * d), ALU.subtract).then_inc(T[f"lev{d}"], 1)
                if not last:
                    dve.tensor_tensor(D_, D_, bank(4 * d + 1), ALU.subtract)
        for d in range(2):
            S_, M, AT, QE, KTL, D_, DT, Y = self.buf[8 * d:8 * d + 8]
            tt = ORDER[d][c]
            dve.drain()
            dve.wait_ge(T[f"ks{d}"], 4 * i + (c + 1))
            vt = b["arena"][:, bass.ds(512 * i + (16384 + 2048 * tt), 512)]
            dve.tensor_tensor(heads(D_), heads(bank(4 * d + 2)), token_scalars(3, d), ALU.mult)
            dve.tensor_tensor(heads(M), heads(vt), token_scalars(1, d), ALU.mult)
            dve.drain()
            dve.tensor_tensor(D_, D_, M, ALU.add).then_inc(T[f"r{d}"], 1)
        for d in range(2):
            S_, M, AT, QE, KTL, D_, DT, Y = self.buf[8 * d:8 * d + 8]
            tok = ORDER[d][c] * 128
            dve.wait_ge(T[f"op{d}"], 4 * i + (c + 1))
            dve.tensor_tensor(heads(S_), heads(S_), spread(small[:, 48 + 4 * d:52 + 4 * d], 128, 2), ALU.mult)
            o = b["arena"][:, bass.ds(2048 * i + 8192, 2048)].rearrange("p (h t) -> p h t", h=4)[:, :, tok:tok + 128]
            if c % 2 == 0:
                dve.tensor_copy(o, heads(bank(4 * d + 1)))
            else:
                dve.tensor_tensor(o, o, heads(bank(4 * d + 1)), ALU.add)
            dve.drain()
            dve.tensor_tensor(S_, S_, bank(4 * d + 2), ALU.add)
            dve.drain().then_inc(T[f"done{d}"], 1)

    def gla_views(self):
        area, h_sb = self.b["area"], self.b["h_sb"]
        self.gq = area(0, 2048, h=4)
        self.gk = area(2048, 2048, h=4)
        self.gv = area(4096, 4096, h=4, t=4)
        self.go = area(8192, 2048, m=8)
        self.glog = area(10240, 4096, d=2, t=4)
        self.gS = [area(14336 + 1024 * d, 1024) for d in range(2)]
        self.gg = area(16384, 2048, m=8)
        self.gb2 = area(18432, 1024, d=2)
        self.gw2 = self.b["arena"][0:16, 19456:20480]
        self.low = self.b["arena"][0:16, 20480:21504]
        self.gbuf = [area(21504 + 512 * n, 512) for n in range(14)]
        self.gbuf2 = [h_sb[:, 512 * n:512 * (n + 1)] for n in range(4)]

    def gla_batch(self, n):
        c, d = divmod(n, 2)
        return c, d, ORDER[d][c], self.gbuf[4 * d:4 * d + 4] + [self.gbuf2[d]]

    def pe_gla(self, pe):
        b, S, T = self.b, self.b["S"], self.S2
        bank, h, w, ident = b["bank"], b["h"], b["w"], b["ident"]
        self.gla_views()
        n0, r0 = b["sched"]["2gla"]
        pe.wait_ge(S["h_ready"], KT * (self.norm1 + 1))
        for c in range(GLA_CHUNKS):
            b["arrived"](pe, n0 + c)
            slot = (n0 + c) % RING
            for half in range(2):
                rho = 2 * c + half
                if r0 + rho >= 4:
                    pe.wait_ge(S["bank_free"], r0 + rho - 3)
                if 4 <= c < 8:
                    for tt in range(2):
                        tok = half * SEQ + tt * 128
                        for k in range(KT):
                            ins = pe.matmul(bank(rho % 4)[:, tt * 256:(tt + 1) * 256], h[:, k, tok:tok + 128],
                                            w[:, slot, k, :], start=k == 0, stop=k == KT - 1)
                    ins.then_inc(S["products"], 1)
                else:
                    tok = TOK if c < 4 else SEQ
                    b["k_products"](pe, bank(rho % 4)[:, 0:tok], lambda k: w[:, slot, k, half * 128:(half + 1) * 128],
                                    lambda k: h[:, k, 0:tok])
        pe.wait_ge(T["loaded_c2"], 80 + 48)
        wl = self.kst[:, 0:256].rearrange("p (k c) -> p k c", k=KT)
        for d in range(2):
            for k in range(KT):
                ins = pe.matmul(bank(4 + d)[0:16, :], wl[:, k, 16 * d:16 * d + 16], h[:, k, :],
                                start=k == 0, stop=k == KT - 1)
        ins.then_inc(T["low_psum"], 1)
        pe.wait_ge(T["low_ready"], 1)
        for n in range(8):
            d, tt = divmod(n, 4)
            if n >= 2:
                pe.wait_ge(T["lg_in"], n - 1)
            pe.matmul(bank(6 + n % 2), self.low[:, d * 512 + tt * 128:d * 512 + tt * 128 + 128],
                      self.gw2[:, d * 512:(d + 1) * 512], start=True, stop=True).then_inc(T["lg_psum"], 1)
        pe.wait_ge(T["gk_ready"], 1)
        pe.wait_ge(S["bank_free"], r0 + 2 * GLA_CHUNKS)
        for n in range(8):
            c, d, tt, (B, TA, KTOK, QE, AT) = self.gla_batch(n)
            if n >= 2:
                pe.wait_ge(T["s_done"], n - 1)
            for hd in range(4):
                ins = pe.matmul(bank(4 * d)[:, hd * 128:(hd + 1) * 128], self.glog[:, d, tt, hd * 128:(hd + 1) * 128],
                                self.tri(d), start=True, stop=True)
            ins.then_inc(T["b_psum"], 1)
            pe.wait_ge(T["kt_fm"], n + 1)
            for hd in range(4):
                ins = pe.transpose(bank(4 * d + 1)[:, hd * 128:(hd + 1) * 128], TA[:, hd * 128:(hd + 1) * 128], ident[:, :])
            ins.then_inc(T["kt_psum"], 1)
            if c >= 2:
                xb = n - 4
                for p in range(LEVELS + 1):
                    m = xb * LEVELS + p
                    if p >= 1:
                        pe.wait_ge(T["w_q"], m)
                        pe.wait_ge(T["w_k"], m)
                    if p >= 2:
                        pe.wait_ge(T["a_read"], xb * (LEVELS + 1) + p - 1)
                    for hd in range(4):
                        if p == 0:
                            lhs, rhs = (a[:, hd, tt * 128:(tt + 1) * 128] for a in (self.gk, self.gq))
                        else:
                            lhs, rhs = (self.gbuf[8 + 2 * (p % 2) + i][:, hd * 128:(hd + 1) * 128] for i in (1, 0))
                        ins = pe.matmul(bank(4 * d + 2 + p % 2)[:, hd * 128:(hd + 1) * 128], lhs, rhs, start=True, stop=True)
                    ins.then_inc(T["a_psum"], 1)
            pe.wait_ge(T["kt_tok"], n + 1)
            if c >= 2:
                pe.wait_ge(T["at_ready"], xb + 1)
                for hd in range(4):
                    for vt in range(2):
                        o = bank(4 * d + 2, 2)[:, (2 * hd + vt) * 128:(2 * hd + vt + 1) * 128]
                        col = hd * 256 + vt * 128
                        pe.matmul(o, self.gS[d][:, col:col + 128], QE[:, hd * 128:(hd + 1) * 128], start=True, stop=False)
                        ins = pe.matmul(o, self.gv[:, hd, tt, vt * 128:(vt + 1) * 128], AT[:, hd * 128:(hd + 1) * 128],
                                        start=False, stop=True)
                if c == 3:
                    ins.then_inc(T["o2_psum"], 1)
            if c < 3:
                for hd in range(4):
                    ins = pe.matmul(bank(4 * d, 2)[:, hd * 256:(hd + 1) * 256], KTOK[:, hd * 128:(hd + 1) * 128],
                                    self.gv[:, hd, tt, :], start=True, stop=True)
                ins.then_inc(T["o2_psum"], 1)
        pe.wait_ge(T["or_sq"], 1)
        sq = b["area"](21504, 2048, h=4, v=2)
        for hd in range(4):
            for vt in range(2):
                ins = pe.matmul(bank(4, 2)[:, hd * 256:(hd + 1) * 256], b["ones"][:, :], sq[:, hd, vt, :],
                                start=vt == 0, stop=vt == 1)
        ins.then_inc(T["or_sum"], 1)
        pe.wait_ge(T["oy_ready"], 1)
        b["pe_residual"](pe, "2out1", self.go, 1, KT, SEQ)

    def act_gla(self, act):
        b, S, T = self.b, self.b["S"], self.S2
        bank = b["bank"]
        self.gla_views()
        n0, r0 = b["sched"]["2gla"]
        for rho in range(2 * GLA_CHUNKS):
            act.wait_ge(S["products"], 2 * n0 + rho + 1)
            if rho < 4:
                act.mul(self.gq[:, rho, :], bank(rho % 4), GLA_DK ** -0.5).then_inc(S["bank_free"], 1)
            elif rho < 8:
                act.copy(self.gk[:, rho - 4, :], bank(rho % 4)).then_inc(S["bank_free"], 1)
            elif rho < 16:
                hd, s = divmod(rho - 8, 2)
                act.copy(self.gv[:, hd, 2 * s:2 * s + 2, :], bank(rho % 4).rearrange("p (t c) -> p t c", t=2))\
                   .then_inc(S["bank_free"], 1)
            else:
                act.activation(self.gg[:, rho - 16, :], bank(rho % 4)[:, 0:SEQ], ACT.Tanh, scale=0.5)\
                   .then_inc(T["gate_tanh"], 1)
        act.wait_ge(T["low_psum"], 1)
        act.copy(self.low.rearrange("p (d c) -> p d c", d=2), bank(4, 2)[0:16].rearrange("p (d c) -> p d c", d=2))\
           .then_inc(T["low_ready"], 1)
        act.wait_ge(T["lg_in"], 8)
        L = b["area"](21504, 4096)
        act.activation(L, L, ACT.Exp)
        act.drain()
        act.activation(L, L, ACT.Ln, bias=1.0).then_inc(T["lg_ln"], 1)
        for n in range(8):
            c, d, tt, (B, TA, KTOK, QE, AT) = self.gla_batch(n)
            act.wait_ge(T["b_psum"], n + 1)
            if n >= 2:
                act.wait_ge(T["s_done"], n - 1)
            act.mul(B, bank(4 * d), 1.0 / 16.0).then_inc(T["b_copied"], 1)
            act.drain()
            act.activation(QE, B, ACT.Exp)
            act.wait_ge(T["kt_arg"], n + 1)
            act.activation(TA, TA, ACT.Exp, scale=-1.0)
            act.drain().then_inc(T["kt_exp"], 1)
            act.wait_ge(T["kt_psum"], n + 1)
            act.copy(KTOK, bank(4 * d + 1)).then_inc(T["kt_tok"], 1)
            if c >= 2:
                xb = n - 4
                for p in range(1, LEVELS + 1):
                    act.wait_ge(T["w_arg"], xb * LEVELS + p)
                    W = self.gbuf[12 + p % 2]
                    act.activation(W, W, ACT.Exp).then_inc(T["w_exp"], 1)
        act.wait_ge(T["or_sum"], 1)
        b["act_rsqrt"](act, b["area"](23552, 1024), bank(4, 2), 1.0 / 256).then_inc(T["or_rinv"], 1)

    def pool_gla(self, pool):
        T = self.S2
        self.gla_views()
        for n in range(4, 8):
            c, d, tt, _ = self.gla_batch(n)
            xb = n - 4
            for p in range(1, LEVELS + 1):
                m = xb * LEVELS + p
                pool.wait_ge(T["w_exp"], m)
                if m >= 3:
                    pool.wait_ge(T["a_psum"], xb * (LEVELS + 1) + p - 1 if p >= 3 else xb * (LEVELS + 1))
                W = self.gbuf[12 + p % 2]
                pool.tensor_tensor(self.gbuf[8 + 2 * (p % 2) + 1].rearrange("p (h c) -> p h c", h=4),
                                   W.rearrange("p (h c) -> p h c", h=4), self.gk[:, :, tt * 128:(tt + 1) * 128],
                                   ALU.mult).then_inc(T["w_k"], 1)

    def dve_gla(self, dve):
        b, S, T = self.b, self.b["S"], self.S2
        bank, spread, small = b["bank"], b["spread"], b["small"]
        self.gla_views()
        n0, r0 = b["sched"]["2gla"]

        def heads(a):
            return a.rearrange("p (h c) -> p h c", h=4)

        for m in range(8):
            dve.wait_ge(T["gate_tanh"], m + 1)
            g = self.gg[:, m, :]
            dve.tensor_scalar(g, g, 0.5, 0.5, ALU.mult, ALU.add)
            dve.drain()
            dve.tensor_tensor(g, g, bank((16 + m) % 4)[:, 0:SEQ], ALU.mult).then_inc(S["bank_free"], 1)
        dve.wait_ge(T["loaded_c2"], 80 + 48)
        L = b["area"](21504, 4096, i=8)
        for n in range(8):
            d, tt = divmod(n, 4)
            dve.wait_ge(T["lg_psum"], n + 1)
            x = self.glog[:, d, tt, :]
            dve.tensor_tensor(x, bank(6 + n % 2), self.gb2[:, d, :], ALU.add)
            dve.drain()
            dve.scalar_tensor_tensor(L[:, n, :], x, -1.0, x, ALU.mult, ALU.min).then_inc(T["lg_in"], 1)
        dve.wait_ge(T["lg_ln"], 1)
        dve.scalar_tensor_tensor(b["area"](10240, 4096), b["area"](10240, 4096), 0.0, b["area"](21504, 4096),
                                 ALU.min, ALU.subtract)
        dve.drain().then_inc(T["gk_ready"], 1)
        for n in range(8):
            c, d, tt, (B, TA, KTOK, QE, AT) = self.gla_batch(n)
            tok = tt * 128
            last = LAST[d]
            el = small[:, 48 + 4 * d:52 + 4 * d]
            q, k = self.gq[:, :, tok:tok + 128], self.gk[:, :, tok:tok + 128]
            dve.wait_ge(T["b_copied"], n + 1)
            dve.tensor_tensor(heads(TA), heads(B), heads(B)[:, :, last:last + 1].to_broadcast([128, 4, 128]), ALU.subtract)\
               .then_inc(T["kt_arg"], 1)
            dve.wait_ge(T["kt_exp"], n + 1)
            dve.tensor_tensor(heads(TA), heads(TA), k, ALU.mult).then_inc(T["kt_fm"], 1)
            dve.drain()
            dve.tensor_copy(el, heads(QE)[:, :, last])
            dve.drain()
            if c >= 2:
                dve.tensor_tensor(heads(QE), heads(QE), q, ALU.mult)
                xb = n - 4

                def weights(p):
                    m = xb * LEVELS + p
                    z = 1 << p
                    W = self.gbuf[12 + p % 2]
                    if m >= 3:
                        dve.wait_ge(T["w_k"], m - 2)
                    Wv, Bv = (a.rearrange("p (n z) -> p n z", z=z) for a in (W, B))
                    ref = Bv[:, :, z // 2 - 1:z // 2].to_broadcast([128, 512 // z, z])
                    dve.drain()
                    dve.tensor_tensor(Wv, Bv, ref, ALU.subtract)
                    dve.drain()
                    dve.scalar_tensor_tensor(W, W, -1.0, W, ALU.mult, ALU.min).then_inc(T["w_arg"], 1)

                weights(1)
                for p in range(LEVELS + 1):
                    if p >= 1:
                        W, QW = self.gbuf[12 + p % 2], self.gbuf[8 + 2 * (p % 2)]
                        dve.wait_ge(T["w_exp"], xb * LEVELS + p)
                        dve.tensor_tensor(heads(QW), heads(W), q, ALU.mult).then_inc(T["w_q"], 1)
                        if p < LEVELS:
                            weights(p + 1)
                    dve.wait_ge(T["a_psum"], xb * (LEVELS + 1) + p + 1)
                    scores = heads(bank(4 * d + 2 + p % 2))
                    if p == 0:
                        dve.tensor_tensor(heads(AT), scores, spread(b["ident"][:, :], 4, 1), ALU.mult)\
                           .then_inc(T["a_read"], 1)
                    else:
                        tmp = self.gbuf2[2]
                        dve.tensor_tensor(heads(tmp), scores, spread(self.lev(d, p - 1), 4, 1), ALU.mult)\
                           .then_inc(T["a_read"], 1)
                        dve.drain()
                        dve.tensor_tensor(AT, AT, tmp, ALU.add)
                    dve.drain()
                dve.drain().then_inc(T["at_ready"], 1)
            dve.wait_ge(T["o2_psum"], n + 1)
            if c >= 2:
                o = self.go[:, :, tok:tok + 128]
                po = bank(4 * d + 2, 2).rearrange("p (m c) -> p m c", m=8)
                if c == 2:
                    dve.tensor_copy(o, po)
                else:
                    dve.tensor_tensor(o, o, po, ALU.add)
            if c < 3:
                Sv = self.gS[d].rearrange("p (h c) -> p h c", h=4)
                if c == 0:
                    dve.tensor_copy(self.gS[d], bank(4 * d, 2))
                else:
                    dve.tensor_tensor(Sv, Sv, spread(el, 256, 2), ALU.mult)
                    dve.drain()
                    dve.tensor_tensor(self.gS[d], self.gS[d], bank(4 * d, 2), ALU.add)
            dve.drain().then_inc(T["s_done"], 1)
        go = b["area"](8192, 2048)
        dve.tensor_tensor(b["area"](21504, 2048), go, go, ALU.mult).then_inc(T["or_sq"], 1)
        dve.wait_ge(T["or_rinv"], 1)
        o4 = b["area"](8192, 2048, h=4, v=2)
        for vt in range(2):
            dve.scalar_tensor_tensor(o4[:, :, vt, :], o4[:, :, vt, :], b["v"]("gla_norm", 1, vt),
                                     b["area"](23552, 1024, h=4), ALU.mult, ALU.mult)
        dve.drain()
        dve.tensor_tensor(go, go, b["area"](16384, 2048), ALU.mult)
        dve.drain().then_inc(T["oy_ready"], 1)
        b["dve_residual"](dve, "2out1", 1, 2, 1)

    def pe_ffn(self, pe, li, norm, tok):
        b, S, T = self.b, self.b["S"], self.S2
        pe.wait_ge(S["h_ready"], KT * (norm + 1))
        self.pe_tiles(pe, f"2up{li}", UP2_CHUNKS, tok)
        pe.wait_ge(T["sq2"], UP2_CHUNKS // 2 * (li + 1))
        b["pe_residual"](pe, f"2down{li}", b["area"](0, FT2 * 512, k=FT2), 4, FT2, tok)

    def act_ffn(self, act, li, tok):
        b, S, T = self.b, self.b["S"], self.S2
        n0, r0 = b["sched"][f"2up{li}"]
        with act.Fori(0, UP2_CHUNKS // 2) as j:
            for q in range(4):
                act.wait_ge(S["products"], 4 * j + (2 * n0 + q + 1))
                act.activation(b["arena"][:, bass.ds(2048 * j + 512 * q, tok)], b["bank"](q)[:, 0:tok], ACT.Relu)\
                   .then_inc(S["bank_free"], 1)

    def dve_ffn(self, dve, li, tok, streams):
        b, S, T = self.b, self.b["S"], self.S2
        n0, r0 = b["sched"][f"2up{li}"]
        with dve.Fori(0, UP2_CHUNKS // 2) as j:
            dve.wait_ge(S["bank_free"], 4 * j + (r0 + 4))
            a = b["arena"][:, bass.ds(2048 * j, 2048)].rearrange("p (q t) -> p q t", q=4)[:, :, 0:tok]
            dve.tensor_tensor(a, a, a, ALU.mult).then_inc(T["sq2"], 1)
        b["dve_residual"](dve, f"2down{li}", 4, 5, streams)

    def pe(self, pe):
        b, S = self.b, self.b["S"]
        self.views()
        b["pe_norm"](pe, 4)
        self.pe_delta(pe)
        for d in range(2):
            pe.wait_ge(self.S2[f"done{d}"], 17)
        self.pe_norms(pe, 4, 4)
        b["pe_norm"](pe, 5)
        pe.wait_ge(S["h_ready"], KT * 6)
        self.pe_tiles(pe, "2z", Z_CHUNKS, TOK)
        pe.wait_ge(self.S2["z_ready"], Z_CHUNKS // 2 + 1)
        b["pe_residual"](pe, "2out0", self.o, 2, 16, TOK)
        b["pe_norm"](pe, 6)
        self.pe_ffn(pe, 0, 6, TOK)
        if LAYERS2 == 2:
            b["pe_ada"](pe, "2ada1", 1, 1)
            b["pe_norm"](pe, self.norm1)
            self.pe_gla(pe)
            b["pe_norm"](pe, self.norm1 + 1)
            self.pe_ffn(pe, 1, self.norm1 + 1, SEQ)

    def act(self, act):
        b, S, T = self.b, self.b["S"], self.S2
        t = b["t"]
        self.views()
        act.wait_ge(T["arena_free"], 1)
        act.dma_start(b["x"][:, :, SEQ:TOK], t["ctx2"].rearrange("p (k c) -> p k c", k=KT)).then_inc(T["loaded_c2"], 16)
        act.dma_start(self.c2[:, :], t["c2"]).then_inc(T["loaded_c2"], 16)
        act.dma_start(self.kst[:, 0:512], t["w_ab"]).then_inc(T["loaded_c2"], 16)
        act.dma_start(b["small"][:, 64:96], t["a_log"]).then_inc(T["loaded_c2"], 16)
        act.dma_start(b["small"][:, 96:128], t["dt_bias"]).then_inc(T["loaded_c2"], 16)
        act.wait_ge(T["loaded_c2"], 80)
        act.wait_ge(S["mods_ready"], 3)
        b["act_norm"](act, 4, 0)
        self.act_delta(act)
        b["act_norm"](act, 6, 1)
        self.act_ffn(act, 0, TOK)
        if LAYERS2 == 2:
            b["act_ada"](act, "2ada1", 1)
            act.wait_ge(S["mods_ready"], self.mods1 + 1)
            act.wait_ge(T["arena_free"], 2)
            act.dma_start(self.kst[:, 0:256], t["w_low"]).then_inc(T["loaded_c2"], 16)
            act.dma_start(b["arena"][0:16, 19456:20480], t["gate_w2"]).then_inc(T["loaded_c2"], 16)
            act.dma_start(b["area"](18432, 1024), t["gate_b2"]).then_inc(T["loaded_c2"], 16)
            b["act_norm"](act, self.norm1, 0)
            self.act_gla(act)
            b["act_norm"](act, self.norm1 + 1, 1)
            self.act_ffn(act, 1, SEQ)

    def pool(self, pool):
        self.views()
        self.pool_delta(pool)
        if LAYERS2 == 2:
            self.pool_gla(pool)

    def dve(self, dve):
        b, S, T = self.b, self.b["S"], self.S2
        self.views()
        dve.drain().then_inc(T["arena_free"], 1)
        b["dve_mods"](dve, 2, "ada_b_20", ("norm_mix_20", "norm_ffn_20"))
        dve.wait_ge(T["loaded_c2"], 80)
        b["dve_norm"](dve, 4)
        self.dve_delta(dve)
        b["dve_residual"](dve, "2out0", 2, 2, 2)
        b["dve_norm"](dve, 6)
        self.dve_ffn(dve, 0, TOK, 2)
        if LAYERS2 == 2:
            b["dve_mods"](dve, self.mods1, "ada_b_21", ("norm_mix_21", "norm_ffn_21"))
            dve.drain().then_inc(T["arena_free"], 1)
            b["dve_norm"](dve, self.norm1)
            self.dve_gla(dve)
            b["dve_norm"](dve, self.norm1 + 1)
            self.dve_ffn(dve, 1, SEQ, 1)
        dve.drain().then_inc(S["x_done"], 1)


def _constants2():
    j, i = np.indices((128, 128))
    tri = [j <= i, j >= i]
    lev = [[], []]
    for level in range(LEVELS):
        s = 1 << level
        m = (j // (2 * s) == i // (2 * s)) & (j % (2 * s) < s) & (i % (2 * s) >= s)
        lev[0].append(m)
        lev[1].append(m.T)
    return np.ascontiguousarray(np.concatenate(tri + lev[0] + lev[1], axis=1).astype(np.float32))


def layout_second(i, stream, out):
    dn = i["dn_w_in_2"][0]
    stream.append(_chunks(dn[:, :6144]))
    stream.append(_chunks(i["dn_w_out_2"][0]))
    stream.append(_chunks(i["ffn_w1_2"][0]))
    stream.append(_chunks(i["ffn_w2_2"][0]))
    out["ctx2"] = _feature_major(i["ctx_2"][0]).reshape(128, KT * SEQ)
    out["c2"] = _constants2()
    out["w_ab"] = dn[:, 6144:].reshape(KT, 128, 64).transpose(1, 0, 2).reshape(128, 512)
    out["a_log"] = np.tile(i["dn_a_log_2"][0].reshape(1, 32), (128, 1))
    out["dt_bias"] = np.tile(i["dn_dt_bias_2"][0].reshape(1, 32), (128, 1))
    if LAYERS2 == 1:
        return
    gl = i["gla_w_in_2"][0]
    stream.append(_chunks(i["ada_w_2"][1]))
    stream.append(_chunks(gl[:, :3072]))
    stream.append(_chunks(i["gla_w_out_2"][0]))
    stream.append(_chunks(i["ffn_w1_2"][1]))
    stream.append(_chunks(i["ffn_w2_2"][1]))
    out["w_low"] = gl[:, 3072:].reshape(KT, 128, 32).transpose(1, 0, 2).reshape(128, 256)
    out["gate_w2"] = i["gla_gate_w2_2"][0].transpose(1, 0, 2).reshape(16, 1024)
    out["gate_b2"] = np.tile(i["gla_gate_b2_2"][0].reshape(1, 1024), (128, 1))


LAYERS2 = 2


def _cols(a):
    return np.asarray(a).reshape(-1, 128).T


def _chunks(wt):
    K, N = wt.shape
    groups = -(-K // D)
    if groups * D != K:
        full = np.zeros((groups * D, N), wt.dtype)
        full[:K] = wt
        wt = full
    a = wt.reshape(groups, KT, 128, N // CHUNK_COLS, CHUNK_COLS).transpose(3, 0, 2, 1, 4)
    return a.reshape(-1, 128, CHUNK)


def _constants1():
    def block_ones(n):
        return np.kron(np.eye(128 // n), np.ones((n, n)))

    rope = np.zeros((128, 128))
    for p in range(128):
        b, d = divmod(p, 32)
        if d < 16:
            rope[32 * b + d + 16, p] = -1.0
        else:
            rope[32 * b + d - 16, p] = 1.0
    n_freq = DIFF_QK // 4
    freqs = np.float32(10000.0) ** (-np.arange(n_freq, dtype=np.float32) / n_freq)
    tok = np.arange(SEQ)
    ang = np.concatenate([(tok // GRID_W).astype(np.float32)[:, None] * freqs,
                          (tok % GRID_W).astype(np.float32)[:, None] * freqs], axis=-1)
    cos = np.tile(np.cos(ang).T, (8, 1))
    sin = np.tile(np.sin(ang).T, (8, 1))
    ntok = 2 * np.pi * (np.outer(tok, tok) % SEQ) / SEQ
    dn = np.concatenate([np.cos(ntok), np.sin(ntok)], axis=1)
    dn = dn.reshape(2, 128, 512).transpose(1, 0, 2).reshape(128, 1024)
    f = np.arange(HEAD)
    nf = 2 * np.pi * (np.outer(f, f) % HEAD) / HEAD
    norm = 1.0 / math.sqrt(SEQ * HEAD)
    dc = np.kron(np.eye(2), np.cos(nf)) * norm
    ds = -np.kron(np.eye(2), np.sin(nf)) * norm
    j = np.arange(GRID_W)
    c0 = np.clip(j - 8, 0, GRID_W - 16)
    inside = (j[None, :] >= c0[:, None]) & (j[None, :] < c0[:, None] + 16)
    namask = np.tile(np.where(inside, 0.0, NEG), (2, 1))
    parts = [block_ones(32), block_ones(64), rope, cos, sin, dn, dc, ds, namask]
    return np.ascontiguousarray(np.concatenate(parts, axis=1).astype(np.float32))


def layout(i, BLOCKS=2):
    stream = []
    for li in range(DEPTH):
        if li == 0:
            stream.append(_chunks(i["w_ada"][0]))
        stream.append(_chunks(i["w_in"][li]))
        stream.append(_chunks(i["w_ada"][1] if li == 0 else i["ada_w_2"][0]))
        stream.append(_chunks(i["w_out"][li]))
        up = i["ffn_up"][li].reshape(D, 2, PAIRS, 256).transpose(0, 2, 1, 3).reshape(D, 2 * D_FF)
        stream.append(_chunks(up))
        stream.append(_chunks(i["ffn_down"][li]))
    vecs = [np.stack([np.stack([_cols(i["c"]), _cols(i["c_ctx"])], 2), np.stack([_cols(i["c_2"]), _cols(i["c_ctx_2"])], 2)],
                     1).reshape(128, 4 * KT)]
    for li in range(DEPTH):
        conv = np.concatenate([i["ffn_conv"][li], i["ffn_conv_b"][li][None]])
        conv = conv.reshape(4, 2, PAIRS, 2, 128).transpose(4, 2, 1, 3, 0).reshape(128, PAIRS * 16)
        def rep(a):
            return np.tile(a, 128 // a.shape[0])[:, None]
        dq, dk, nq, nk = (rep(i[n][li]) for n in ("diff_qn", "diff_kn", "na_qn", "na_kn"))
        vecs += [_cols(i["b_ada"][li]), _cols(i["g_mix"][li]), _cols(i["g_ffn"][li]), conv,
                 dq, dq, dk, dk, nq, nq, nk, nk, rep(i["diff_subln"][li]), _cols(i["gmlp_norm"][li])]
    for li in range(DEPTH):
        vecs += [_cols(i["ada_b_2"][li]), _cols(i["norm_mix_g_2"][li]), _cols(i["norm_ffn_g_2"][li])]
    vecs += [i["dn_conv_w_2"][0].reshape(32, 128, 5).transpose(1, 0, 2).reshape(128, 160),
             _cols(i["dn_norm_g_2"][0]), _cols(i["gla_norm_g_2"][0])]
    vec = np.concatenate(vecs, axis=1)
    assert vec.shape[1] == VEC["end"]
    d1 = [np.tile(i["diff_lam"][li].reshape(1, 128), (128, 1)) for li in range(DEPTH)]
    d1 += [i["gmlp_ws"][li].transpose(2, 0, 1).reshape(128, 512) for li in range(DEPTH)]
    d1 += [np.repeat(i["gmlp_b"][li].reshape(2, 2, 128).transpose(1, 0, 2), 64, axis=0).reshape(128, 256) for li in range(DEPTH)]
    xx = np.concatenate([_feature_major(i["x"][0]), _feature_major(i["ctx"][0])], axis=2).reshape(128, KT * TOK)
    out = {"x": xx, "vec": vec, "ident": np.eye(128, dtype=np.float32), "ones": np.ones((128, 128), np.float32),
           "c1": _constants1(), "d1": np.concatenate(d1, axis=1), "rpb": np.repeat(i["na_rpb"][:, :, None], GRID_W, axis=2).reshape(-1)}
    if BLOCKS == 2:
        layout_second(i, stream, out)
    out["stream"] = np.concatenate(stream)
    return {k: np.ascontiguousarray(a) for k, a in out.items()}


def _feature_major(a):
    return np.asarray(a).T.reshape(KT, 128, -1).transpose(1, 0, 2)


BLOCKS = 2


def kernel(**inputs):
    import concourse.bacc as bacc
    from concourse.bass_utils import run_bass_kernel_spmd as run

    nc = bacc.Bacc("TRN2", target_bir_lowering=False, num_devices=1)
    arrays = layout({k: np.asarray(a) for k, a in inputs.items()}, BLOCKS)
    t = {n: nc.dram_tensor(f"in_{n}", a.shape, mybir.dt.from_np(a.dtype), kind="ExternalInput").ap()
         for n, a in arrays.items()}
    out = nc.dram_tensor("out", (128, KT * SEQ), F32, kind="ExternalOutput").ap()
    build_program(nc, t, out, BLOCKS)
    r = run(nc, [{f"in_{n}": a for n, a in arrays.items()}], core_ids=[0])
    got = r.results[0]["out"].reshape(128, KT, SEQ)
    return got.transpose(1, 0, 2).reshape(D, SEQ).T.reshape(1, SEQ, D)
```
